# Optimizing a Trainium2 kernel written in Bass

```python
import math
import jax, jax.numpy as jnp
from jax import lax
import numpy as np

D_MODEL = 2048
BATCH = 1
SEQ = 256
DEPTH = 1

CHUNK = 64

D_MIX = D_MODEL
D_LRU = D_MIX // 2
D_CONV = D_MIX - D_LRU
LRU_HEADS = 16
LRU_HEAD_DIM = D_LRU // LRU_HEADS
LRU_C = 8.0
LRU_CONV_W = 4
CONF_GROUPS = 16
CONF_CONV_W = 31
N_GROUPS = 4
EXPERTS_PER_GROUP = 8
TOP_K = 2
D_EXPERT = D_MODEL // 4
LN_EPS = 1e-5
DN_ALPHA = (2 * DEPTH) ** 0.25
DN_BETA = (8 * DEPTH) ** -0.25

kernel_name = "hymba_rglru_conformer_hiermoe_deepnorm"

def layer_norm(x, g, b):
    xf = x.astype(jnp.float32)
    mu = jnp.mean(xf, axis=-1, keepdims=True)
    var = jnp.mean(jnp.square(xf - mu), axis=-1, keepdims=True)
    y = (xf - mu) * lax.rsqrt(var + LN_EPS) * g.astype(jnp.float32) + b.astype(jnp.float32)
    return y.astype(x.dtype)

def causal_depthwise_conv(x, w, b):
    k, c = w.shape
    y = lax.conv_general_dilated(
        x, w[:, None, :].astype(x.dtype), window_strides=(1,), padding=[(k - 1, 0)],
        dimension_numbers=("NWC", "WIO", "NWC"), feature_group_count=c)
    return y + b.astype(x.dtype)

def rg_lru(x, w_a, b_a, w_x, b_x, lam):
    bsz, t, c = x.shape
    xh = x.reshape(bsz, t, LRU_HEADS, LRU_HEAD_DIM)
    r = jax.nn.sigmoid(jnp.einsum("bthi,hij->bthj", xh, w_a).reshape(bsz, t, c) + b_a)
    i = jax.nn.sigmoid(jnp.einsum("bthi,hij->bthj", xh, w_x).reshape(bsz, t, c) + b_x)
    log_a = -LRU_C * r.astype(jnp.float32) * jax.nn.softplus(-lam.astype(jnp.float32))
    a = jnp.exp(log_a)
    u = jnp.sqrt(-jnp.expm1(2.0 * log_a)) * (i * x).astype(jnp.float32)

    def combine(left, right):
        a1, b1 = left
        a2, b2 = right
        return a1 * a2, a2 * b1 + b2

    _, h = lax.associative_scan(combine, (a, u), axis=1)
    return h.astype(x.dtype)

def hier_moe(x, wg, bg, we, be, w_gate, w_up, w_down):
    bsz, t, _ = x.shape
    lg = (jnp.einsum("btd,dg->btg", x, wg) + bg).astype(jnp.float32)
    pg = jax.nn.softmax(lg, axis=-1)
    pg_top, g_sel = lax.top_k(pg, 1)
    le = (jnp.einsum("btd,de->bte", x, we) + be).astype(jnp.float32)
    le = le.reshape(bsz, t, N_GROUPS, EXPERTS_PER_GROUP)
    le_sel = jnp.take_along_axis(le, g_sel[..., None], axis=2)[:, :, 0]
    top_v, top_i = lax.top_k(le_sel, TOP_K)
    q = jax.nn.softmax(top_v, axis=-1) * pg_top
    w_e = jnp.sum(jax.nn.one_hot(top_i, EXPERTS_PER_GROUP, dtype=jnp.float32) * q[..., None], axis=-2)
    w_full = jax.nn.one_hot(g_sel[..., 0], N_GROUPS, dtype=jnp.float32)[..., None] * w_e[:, :, None, :]
    w_full = w_full.astype(x.dtype)
    y = jnp.zeros_like(x)
    for g in range(N_GROUPS):
        h = jax.nn.silu(jnp.einsum("btd,edf->btef", x, w_gate[g])) * jnp.einsum("btd,edf->btef", x, w_up[g])
        y = y + jnp.einsum("btef,efd->btd", h * w_full[:, :, g, :, None], w_down[g])
    return y

def setup_inputs(seed: int = 0) -> dict:
    key = jax.random.key(seed)
    ks = jax.random.split(key, 32)
    f32 = jnp.float32
    L = DEPTH
    G, E, F = N_GROUPS, EXPERTS_PER_GROUP, D_EXPERT

    def nrm(k, shape, scale):
        return jax.random.normal(k, shape, f32) * scale

    u = jax.random.uniform(ks[10], (L, D_LRU), f32, 0.9, 0.999)
    s = u ** (1.0 / LRU_C)
    return {
        "x": nrm(ks[0], (BATCH, SEQ, D_MODEL), 1.0),
        "ln_in_g": 1.0 + nrm(ks[1], (D_MODEL,), 0.02),
        "ln_in_b": nrm(ks[2], (D_MODEL,), 0.02),
        "w_in": nrm(ks[3], (L, D_MODEL, 2 * D_LRU + 2 * D_CONV), D_MODEL ** -0.5),
        "lru_conv_w": nrm(ks[4], (L, LRU_CONV_W, D_LRU), LRU_CONV_W ** -0.5),
        "lru_conv_b": nrm(ks[5], (L, D_LRU), 0.02),
        "lru_w_a": nrm(ks[6], (L, LRU_HEADS, LRU_HEAD_DIM, LRU_HEAD_DIM), LRU_HEAD_DIM ** -0.5),
        "lru_b_a": nrm(ks[7], (L, D_LRU), 0.02),
        "lru_w_x": nrm(ks[8], (L, LRU_HEADS, LRU_HEAD_DIM, LRU_HEAD_DIM), LRU_HEAD_DIM ** -0.5),
        "lru_b_x": nrm(ks[9], (L, D_LRU), 0.02),
        "lru_lambda": jnp.log(s) - jnp.log1p(-s),
        "conf_conv_w": nrm(ks[11], (L, CONF_CONV_W, D_CONV), CONF_CONV_W ** -0.5),
        "conf_conv_b": nrm(ks[12], (L, D_CONV), 0.02),
        "conf_ln_g": 1.0 + nrm(ks[13], (L, D_CONV), 0.02),
        "conf_ln_b": nrm(ks[14], (L, D_CONV), 0.02),
        "w_out": nrm(ks[15], (L, D_MIX, D_MODEL), D_MIX ** -0.5 * DN_BETA),
        "ln1_g": 1.0 + nrm(ks[16], (L, D_MODEL), 0.02),
        "ln1_b": nrm(ks[17], (L, D_MODEL), 0.02),
        "router_group_w": nrm(ks[18], (L, D_MODEL, G), D_MODEL ** -0.5),
        "router_group_b": nrm(ks[19], (L, G), 0.01),
        "router_expert_w": nrm(ks[20], (L, D_MODEL, G * E), D_MODEL ** -0.5),
        "router_expert_b": nrm(ks[21], (L, G * E), 0.01),
        "exp_w_gate": nrm(ks[22], (L, G, E, D_MODEL, F), D_MODEL ** -0.5),
        "exp_w_up": nrm(ks[23], (L, G, E, D_MODEL, F), D_MODEL ** -0.5),
        "exp_w_down": nrm(ks[24], (L, G, E, F, D_MODEL), F ** -0.5 * DN_BETA),
        "ln2_g": 1.0 + nrm(ks[25], (L, D_MODEL), 0.02),
        "ln2_b": nrm(ks[26], (L, D_MODEL), 0.02),
    }

def reference(x, ln_in_g, ln_in_b, w_in, lru_conv_w, lru_conv_b, lru_w_a, lru_b_a,
              lru_w_x, lru_b_x, lru_lambda, conf_conv_w, conf_conv_b, conf_ln_g, conf_ln_b,
              w_out, ln1_g, ln1_b, router_group_w, router_group_b, router_expert_w,
              router_expert_b, exp_w_gate, exp_w_up, exp_w_down, ln2_g, ln2_b):
    h = layer_norm(x, ln_in_g, ln_in_b)
    for l in range(DEPTH):
        z = jnp.einsum("btd,dc->btc", h, w_in[l])
        lru_x = z[..., :D_LRU]
        lru_g = z[..., D_LRU:2 * D_LRU]
        conf_v = z[..., 2 * D_LRU:2 * D_LRU + D_CONV]
        conf_g = z[..., 2 * D_LRU + D_CONV:]
        a_in = causal_depthwise_conv(lru_x, lru_conv_w[l], lru_conv_b[l])
        a_out = jax.nn.gelu(lru_g, approximate=True) * rg_lru(
            a_in, lru_w_a[l], lru_b_a[l], lru_w_x[l], lru_b_x[l], lru_lambda[l])
        b_in = conf_v * jax.nn.sigmoid(conf_g)
        b_c = causal_depthwise_conv(b_in, conf_conv_w[l], conf_conv_b[l])
        b_out = jax.nn.silu(layer_norm(b_c, conf_ln_g[l], conf_ln_b[l]))
        mix = jnp.einsum("btc,cd->btd", jnp.concatenate([a_out, b_out], axis=-1), w_out[l])
        h = layer_norm(DN_ALPHA * h + mix, ln1_g[l], ln1_b[l])
        ffn = hier_moe(h, router_group_w[l], router_group_b[l], router_expert_w[l],
                       router_expert_b[l], exp_w_gate[l], exp_w_up[l], exp_w_down[l])
        h = layer_norm(DN_ALPHA * h + ffn, ln2_g[l], ln2_b[l])
    return h


_drawn_inputs = setup_inputs


def setup_inputs(seed=0):
    import zlib

    import numpy as np

    out = dict(_drawn_inputs(seed))
    spreads = {}
    factors = {'lru_b_a': 64.0,
     'lru_b_x': 64.0,
     'conf_conv_b': 4.98,
     'conf_ln_g': 7.349,
     'conf_ln_b': 20.042,
     'router_group_b': 21.624,
     'router_expert_b': 24.625,
     'ln2_g': 20.393,
     'ln2_b': 21.606,
     'lru_conv_b': 3.896}
    for name, (base, spread) in spreads.items():
        noise = np.random.default_rng([zlib.crc32(name.encode()), seed]).standard_normal(out[name].shape)
        drawn = base * np.exp(spread * noise) if base else spread * noise
        out[name] = __import__('jax').numpy.asarray(drawn.astype(out[name].dtype))
    for name, factor in factors.items():
        out[name] = (out[name] * factor).astype(out[name].dtype)
    return out
```

```python
from contextlib import ExitStack

import concourse.bass as bass
from concourse import mybir

D = 2048
SEQ = 256
P = 128
TT = SEQ // P
KD = D // P
HALF = D // 2
CT = HALF // P
LRU_TAPS = 4
CONF_TAPS = 31
HEAD = 64
GROUPS = 4
PER_GROUP = 8
EXPERTS = GROUPS * PER_GROUP
F = D // 4
SLOTS = 64
PASSES = SEQ // SLOTS
ALPHA = 2.0 ** 0.25
EPS = 1e-5
LRU_C = 8.0

RING = 8
SLOT = 4096
MIX_RING = 4
CHUNK = SLOT // KD
PAIRS = HALF // CHUNK
OUT_CHUNKS = D // CHUNK
MIX_USES = (4 * PAIRS + OUT_CHUNKS) // MIX_RING
PIECES = 6
GU_PIECES = 4
DOWN_PIECES = PIECES - GU_PIECES
KP = KD // GU_PIECES
UNROLL = 4
TURNS = UNROLL * PIECES // RING
LOOPS = EXPERTS // UNROLL
GATHERS = EXPERTS + 1
ROUNDS = 4
SCATTERS = ROUNDS * GATHERS

R_LNG, R_LNB = 0, KD
R_LCW = 2 * KD
R_LCB = R_LCW + LRU_TAPS * CT
R_BA, R_BX, R_LAM = R_LCB + CT, R_LCB + 2 * CT, R_LCB + 3 * CT
R_CCB, R_CLG, R_CLB = R_LCB + 4 * CT, R_LCB + 5 * CT, R_LCB + 6 * CT
ROWS_A = R_LCB + 7 * CT
R_CCW = ROWS_A
TAP_ROWS = CONF_TAPS * CT


def build(nc, io, out):
    f32 = mybir.dt.float32
    i32 = mybir.dt.int32
    ALU = mybir.AluOpType
    ACT = mybir.ActivationFunctionType
    AX = mybir.AxisListType

    ctx = ExitStack()
    with ctx:
        def sb(name, shape, dt=f32):
            return ctx.enter_context(nc.sbuf_tensor(name, shape, dt))

        def sem(name):
            return ctx.enter_context(nc.semaphore(name))

        ring = sb("ring", [P, RING, SLOT])
        rows = sb("rows", [P, TT, D])
        turned = sb("turned", [P, KD * SEQ])
        region = sb("region", [P, KD * SEQ])
        scaling = sb("scaling", [P, 2 * D])
        ident = sb("ident", [P, P])
        mean_w = sb("mean_w", [P, P])
        before = sb("before", [P, P])
        ones = sb("ones", [P, P])
        slot_id = sb("slot_id", [P, 2 * SLOTS])
        router_w = sb("router_w", [P, KD, GROUPS + EXPERTS])
        router_b = sb("router_b", [P, GROUPS + EXPERTS])
        eps = sb("eps", [P, 1])
        stats = sb("stats", [P, TT, 8, 6])
        moments = sb("moments", [P, TT, 2])
        rstd = sb("rstd", [P, TT])
        rank = sb("rank", [P, TT, GATHERS])
        weight = sb("weight", [P, TT, GATHERS])
        mask = sb("mask", [P, TT, EXPERTS])[:, :, :]
        more = sb("more", [1, PASSES], i32)
        rt = sb("rt", [P, 512])
        psum = ctx.enter_context(nc.psum_tensor("psum", [P, 8, 512], f32))

        h_t = turned[:, :].rearrange("p (k t) -> p k t", k=KD)
        mix_t = region[:, :].rearrange("p (k t) -> p k t", k=KD)
        total = region[:, :].rearrange("p (t d) -> p t d", t=TT)
        gain = scaling[:, 0:D]
        shift = scaling[:, D:2 * D]
        gain2 = turned[:, 0:D]
        shift2 = turned[:, D:2 * D]

        scratch = ring[:, MIX_RING:RING, :].rearrange("p s f -> p (s f)")
        used = [0]

        def tmp(*shape):
            n = 1
            for s in shape:
                n *= s
            a = used[0]
            used[0] = a + n
            assert used[0] <= (RING - MIX_RING) * SLOT
            v = scratch[:, a:a + n]
            if len(shape) == 2:
                return v.rearrange("p (a b) -> p a b", a=shape[0])
            if len(shape) == 3:
                return v.rearrange("p (a b c) -> p a b c", a=shape[0], b=shape[1])
            return v

        raw_a = tmp(P)
        raw_t = tmp(2, P)
        chan = tmp(ROWS_A + TAP_ROWS)
        decay = tmp(8, CT)
        w_a = tmp(CT, P)
        w_x = tmp(CT, P)
        glu = tmp(2, 2, SEQ + CONF_TAPS - 1)
        conf_sig = tmp(2, SEQ)
        conv = tmp(CT, SEQ)
        square = tmp(CT, SEQ)
        conf_rstd = tmp(SEQ)
        lru_in = tmp(2, 2, SEQ + LRU_TAPS - 1)
        a_in = tmp(2, 2, SEQ)
        gelu = tmp(2, 2, SEQ)
        r_gate, i_gate, a_dec, a_sq, a_th, drive, state = (tmp(2, SEQ) for _ in range(7))

        e_used = [0]

        def etmp(*shape):
            n = 1
            for s in shape:
                n *= s
            a = e_used[0]
            e_used[0] = a + n
            assert e_used[0] <= 2 * D
            v = scaling[:, a:a + n]
            if len(shape) == 2:
                return v.rearrange("p (a b) -> p a b", a=shape[0])
            return v

        xg = etmp(KD, SLOTS)
        pick = etmp(TT, SLOTS)
        pick_w = etmp(TT, 2 * SLOTS)
        place = etmp(2, SEQ)
        sig = etmp(F // 2)
        hid = etmp(F // 2)
        hid_t = etmp(2, P)
        y_sb = etmp(2, 512)

        x_here = [sem(f"x_here{t}") for t in range(TT)]
        gain_used = sem("gain_used")
        params_here = sem("params_here")
        gates_here = sem("gates_here")
        gain_here = [sem(f"gain_here{i}") for i in range(3)]
        arrived = [sem(f"arrived{s}") for s in range(RING)]
        consts = sem("consts")
        zeroed = sem("zeroed")
        params_turned = sem("params_turned")
        chan_ready = sem("chan_ready")
        vec = sem("vec")
        sca = sem("sca")
        var_ready = sem("var_ready")
        root_ready = sem("root_ready")
        norm_ready = sem("norm_ready")
        h_turned = sem("h_turned")
        ht_act = sem("ht_act")
        ht_vec = sem("ht_vec")
        z_ready = sem("z_ready")
        conf_sig_ready = sem("conf_sig_ready")
        glu_ready = sem("glu_ready")
        conv_ready = sem("conv_ready")
        mean_ready = sem("mean_ready")
        centred = sem("centred")
        square_ready = sem("square_ready")
        cvar_ready = sem("cvar_ready")
        conf_root = sem("conf_root")
        conf_normed = sem("conf_normed")
        conf_done = sem("conf_done")
        rates_in = sem("rates_in")
        rates_exp = sem("rates_exp")
        rates_ready = sem("rates_ready")
        lru_in_ready = sem("lru_in_ready")
        gelu_ready = sem("gelu_ready")
        a_in_ready = sem("a_in_ready")
        gates_ready = sem("gates_ready")
        decays_ready = sem("decays_ready")
        square1_ready = sem("square1_ready")
        scale_ready = sem("scale_ready")
        lru_done = sem("lru_done")
        out_ready = sem("out_ready")
        out_taken = sem("out_taken")
        h2_ready = sem("h2_ready")
        h2_turned = sem("h2_turned")
        h2t_act = sem("h2t_act")
        h2t_vec = sem("h2t_vec")
        logits_ready = sem("logits_ready")
        exps_in = sem("exps_in")
        exps_ready = sem("exps_ready")
        masks_ready = sem("masks_ready")
        ranks_ready = sem("ranks_ready")
        more_ready = sem("more_ready")
        onehot_ready = sem("onehot_ready")
        xg_gathered = sem("xg_gathered")
        xg_copied = sem("xg_copied")
        q_turned = sem("q_turned")
        q_copied = sem("q_copied")
        gu_used = sem("gu_used")
        silu_done = sem("silu_done")
        hid_ready = sem("hid_ready")
        hid_turned = sem("hid_turned")
        hid_copied = sem("hid_copied")
        down_used = sem("down_used")
        y_copied = sem("y_copied")
        scattered = sem("scattered")
        added = sem("added")
        out_part = sem("out_part")
        stored = sem("stored")

        x_v = io["x"].rearrange("b (t p) d -> (b t) p d", p=P)
        out_v = out.rearrange("b (t p) d -> (b t) p d", p=P)
        w_in_v = io["w_in"].rearrange("l (k p) c -> (l p) k c", p=P)
        w_out_v = io["w_out"].rearrange("l (k p) c -> (l p) k c", p=P)
        w_gate_v = io["exp_w_gate"].rearrange("l g e (q k p) f -> (l g e) q p k f", p=P, k=KP)
        w_up_v = io["exp_w_up"].rearrange("l g e (q k p) f -> (l g e) q p k f", p=P, k=KP)
        w_down_v = io["exp_w_down"].rearrange("l g e (h c p) d -> (l g e) h c p d", p=P, c=2)
        gu_slot = [ring[:, s, :].rearrange("p (w k f) -> p w k f", w=2, k=KP) for s in range(RING)]
        down_slot = [ring[:, s, :].rearrange("p (c d) -> p c d", c=2) for s in range(RING)]
        mix_slot = [ring[:, s, :].rearrange("p (k c) -> p k c", k=KD) for s in range(MIX_RING)]

        in_cols = ([q * HALF + CHUNK * i for i in range(PAIRS) for q in (2, 3)]
                   + [q * HALF + CHUNK * i for i in range(PAIRS) for q in (0, 1)])

        block = ctx.enter_context(nc.Block())

        @block.sync
        def _(sp):
            for t in range(TT):
                sp.dma_start(rows[:, t, :], x_v[t]).then_inc(x_here[t], 16)
            for i, c in enumerate(in_cols):
                if i >= MIX_RING:
                    sp.wait_ge(z_ready, i - MIX_RING + 1)
                sp.dma_start(mix_slot[i % MIX_RING], w_in_v[:, :, c:c + CHUNK]).then_inc(arrived[i % MIX_RING], 16)
            for n in range(OUT_CHUNKS):
                i = len(in_cols) + n
                if n < MIX_RING:
                    sp.wait_ge(z_ready, i - MIX_RING + 1)
                else:
                    sp.wait_ge(out_ready, n - MIX_RING + 1)
                sp.dma_start(mix_slot[i % MIX_RING], w_out_v[:, :, n * CHUNK:(n + 1) * CHUNK]).then_inc(arrived[i % MIX_RING], 16)

            def load_piece(first, j, n):
                s = j % RING
                expert = first + j // PIECES
                old, q = (j - RING) // PIECES, (j - RING) % PIECES
                if isinstance(n, int) and j < MIX_RING:
                    sp.wait_ge(out_ready, OUT_CHUNKS - MIX_RING + s + 1)
                elif isinstance(n, int) and j < RING:
                    sp.wait_ge(lru_done, PAIRS)
                elif q < GU_PIECES:
                    sp.wait_ge(gu_used, (n + old) * GU_PIECES + q + 1)
                else:
                    sp.wait_ge(down_used, (n + old) * DOWN_PIECES + q - GU_PIECES + 1)
                q = j % PIECES
                if q < GU_PIECES:
                    for w, src in enumerate((w_gate_v, w_up_v)):
                        sp.dma_start(gu_slot[s][:, w], src[bass.ds(expert, 1), q].rearrange(
                            "o p k f -> (o p) k f")).then_inc(arrived[s], 16)
                else:
                    for c in range(2):
                        sp.dma_start(down_slot[s][:, c], w_down_v[bass.ds(expert, 1), q - GU_PIECES, c].rearrange(
                            "o p d -> (o p) d")).then_inc(arrived[s], 16)

            for j in range(UNROLL * PIECES):
                load_piece(0, j, 0)
            with sp.Fori(1, LOOPS) as g:
                for j in range(UNROLL * PIECES):
                    load_piece(g * UNROLL, j, g * UNROLL)
            sp.wait_ge(more_ready, 1)
            with sp.Fori(1, PASSES) as p:
                needed = sp.value_load(more[0:1, bass.ds(p, 1)], min_val=0, max_val=1)
                with sp.If(needed > 0):
                    with sp.Fori(0, LOOPS) as g:
                        for j in range(UNROLL * PIECES):
                            load_piece(g * UNROLL, j, p * EXPERTS + g * UNROLL)
            for t in range(TT):
                sp.wait_ge(out_part, t + 1)
                sp.dma_start(out_v[t], total[:, t, :]).then_inc(stored, 16)
            sp.wait_ge(stored, 16 * TT)

        @block.gpsimd
        def _(pool):
            nc.gpsimd.memset(ident[:, :], 0.0)
            nc.gpsimd.memset(before[:, :], 1.0).then_inc(zeroed, 1)
            pool.wait_ge(zeroed, 1)
            nc.gpsimd.affine_select(out=ident[:, :], in_=ident[:, :], compare_op=ALU.not_equal, fill=1.0,
                                    base=0, pattern=[[-1, P]], channel_multiplier=1)
            nc.gpsimd.affine_select(out=before[:, :], in_=before[:, :], compare_op=ALU.is_gt, fill=0.0,
                                    base=0, pattern=[[1, P]], channel_multiplier=-1)
            nc.gpsimd.memset(eps[:, :], EPS).then_inc(consts, 1)
            nc.gpsimd.memset(w_a, 0.0)
            nc.gpsimd.memset(w_x, 0.0).then_inc(zeroed, 1)
            nc.gpsimd.memset(glu[:, :, :, 0:CONF_TAPS - 1], 0.0)
            nc.gpsimd.memset(lru_in[:, :, :, 0:LRU_TAPS - 1], 0.0)
            nc.gpsimd.memset(ones[:, :], 1.0)
            nc.gpsimd.memset(mean_w[:, :], 1.0 / HALF)
            nc.gpsimd.iota(slot_id[:, :], pattern=[[0, 2], [1, SLOTS]], base=0, channel_multiplier=0,
                           allow_small_or_imprecise_dtypes=True)
            nc.gpsimd.iota(rt[:, 0:EXPERTS], pattern=[[1, EXPERTS]], base=0, channel_multiplier=0,
                           allow_small_or_imprecise_dtypes=True).then_inc(consts, 1)
            pool.wait_ge(gain_used, 1)
            pool.dma_start(gain, io["ln1_g"][0].partition_broadcast(P)).then_inc(gain_here[1], 16)
            pool.dma_start(shift, io["ln1_b"][0].partition_broadcast(P)).then_inc(gain_here[1], 16)
            pool.wait_ge(h2_ready, TT)
            nc.gpsimd.memset(y_sb, 0.0).then_inc(y_copied, 1)
            for t in range(TT):
                pool.wait_ge(h2_ready, t + 1)
                ins = nc.gpsimd.tensor_scalar(out=total[:, t, :], in0=rows[:, t, :], scalar1=ALPHA, scalar2=0.0,
                                              op0=ALU.mult, op1=ALU.add)
            ins.then_inc(added, 1)
            pool.wait_ge(logits_ready, 1)
            pool.dma_start(gain2, io["ln2_g"][0].partition_broadcast(P)).then_inc(gain_here[2], 16)
            pool.dma_start(shift2, io["ln2_b"][0].partition_broadcast(P)).then_inc(gain_here[2], 16)

        @block.scalar
        def _(act):
            def load_rows(name, r, n):
                src = io[name]
                src = src.rearrange("(c q) -> c q", q=P) if len(src.shape) == 1 else (
                    src.rearrange("l (c q) -> (l c) q", q=P) if len(src.shape) == 2 else
                    src.rearrange("l k (c q) -> (l k c) q", q=P))
                act.dma_start(raw_a[r:r + n, :], src).then_inc(params_here, 16)

            loaded = [("ln_in_g", R_LNG, KD), ("ln_in_b", R_LNB, KD), ("lru_conv_w", R_LCW, LRU_TAPS * CT),
                      ("lru_conv_b", R_LCB, CT), ("lru_b_a", R_BA, CT), ("lru_b_x", R_BX, CT),
                      ("lru_lambda", R_LAM, CT), ("conf_conv_b", R_CCB, CT), ("conf_ln_g", R_CLG, CT),
                      ("conf_ln_b", R_CLB, CT)]
            for name, r, n in loaded:
                load_rows(name, r, n)
            taps = io["conf_conv_w"].rearrange("l k (c q) -> (l k c) q", q=P)
            act.dma_start(raw_t[:, 0, :], taps[0:P]).then_inc(params_here, 16)
            act.dma_start(raw_t[0:TAP_ROWS - P, 1, :], taps[P:TAP_ROWS]).then_inc(params_here, 16)
            act.dma_start(gain, io["ln_in_g"].partition_broadcast(P)).then_inc(gain_here[0], 16)
            act.dma_start(shift, io["ln_in_b"].partition_broadcast(P)).then_inc(gain_here[0], 16)
            act.dma_start(router_w[:, :, 0:GROUPS], io["router_group_w"].rearrange("l (k p) g -> (l p) k g", p=P)).then_inc(gates_here, 16)
            act.dma_start(router_w[:, :, GROUPS:], io["router_expert_w"].rearrange("l (k p) g -> (l p) k g", p=P)).then_inc(gates_here, 16)
            act.dma_start(router_b[:, 0:GROUPS], io["router_group_b"][0].partition_broadcast(P)).then_inc(gates_here, 16)
            act.dma_start(router_b[:, GROUPS:], io["router_expert_b"][0].partition_broadcast(P)).then_inc(gates_here, 16)
            act.wait_ge(zeroed, 2)
            for dst, name in ((w_a, "lru_w_a"), (w_x, "lru_w_x")):
                for b in range(2):
                    src = io[name].rearrange("l (c b) i j -> (l b) i c j", b=2)[b]
                    act.dma_start(dst[b * HEAD:(b + 1) * HEAD, :, b * HEAD:(b + 1) * HEAD], src).then_inc(gates_here, 16)

            act.wait_ge(consts, 1)
            for t in range(TT):
                act.wait_ge(var_ready, t + 1)
                nc.scalar.activation(rstd[:, t:t + 1], moments[:, t, 1:2], ACT.Sqrt, bias=eps[:, 0:1]).then_inc(root_ready, 1)
            act.wait_ge(params_turned, 1)
            nc.scalar.copy(chan[:, 0:ROWS_A + TAP_ROWS], psum[:, 3, 0:ROWS_A + TAP_ROWS]).then_inc(chan_ready, 1)
            act.wait_ge(chan_ready, 1)
            for f in range(0, 2 * TT * 2, 2):
                act.wait_ge(h_turned, f + 1)
                for k in range(4):
                    kk = 4 * (f % 4) + k
                    ins = nc.scalar.activation(h_t[:, kk, (f // 4) * P:(f // 4 + 1) * P], psum[:, 4 + f % 4, k * P:(k + 1) * P],
                                               ACT.Identity, bias=chan[:, R_LNB + kk:R_LNB + kk + 1],
                                               scale=chan[:, R_LNG + kk:R_LNG + kk + 1])
                ins.then_inc(ht_act, 1)
            act.wait_ge(rates_in, 1)
            nc.scalar.activation(decay[:, 1, :], decay[:, 0, :], ACT.Exp).then_inc(rates_exp, 1)
            for i in range(PAIRS):
                act.wait_ge(z_ready, 2 * i + 2)
                if i >= 1:
                    act.wait_ge(glu_ready, i)
                nc.scalar.activation(conf_sig, psum[:, (2 * i + 1) % 4, :].rearrange("p (a b) -> p a b", a=2),
                                     ACT.Sigmoid).then_inc(conf_sig_ready, 1)

            def lru_front(i):
                b = i % 2
                act.wait_ge(z_ready, 2 * PAIRS + 2 * i + 1)
                if i >= 2:
                    act.wait_ge(a_in_ready, i - 1)
                nc.scalar.copy(lru_in[:, b, :, LRU_TAPS - 1:], psum[:, (2 * i) % 4, :].rearrange(
                    "p (a b) -> p a b", a=2)).then_inc(lru_in_ready, 1)
                act.wait_ge(z_ready, 2 * PAIRS + 2 * i + 2)
                if i >= 2:
                    act.wait_ge(lru_done, i - 1)
                nc.scalar.activation(gelu[:, b], psum[:, (2 * i + 1) % 4, :].rearrange("p (a b) -> p a b", a=2),
                                     ACT.Gelu_apprx_tanh).then_inc(gelu_ready, 1)
                act.wait_ge(gates_ready, i + 1)
                if i >= 1:
                    act.wait_ge(lru_done, i)
                for c in range(2):
                    cc = 2 * i + c
                    nc.scalar.activation(r_gate[:, c], psum[:, 4, c * SEQ:(c + 1) * SEQ], ACT.Sigmoid,
                                         bias=chan[:, R_BA + cc:R_BA + cc + 1]).then_inc(sca, 1)
                    nc.scalar.activation(i_gate[:, c], psum[:, 5, c * SEQ:(c + 1) * SEQ], ACT.Sigmoid,
                                         bias=chan[:, R_BX + cc:R_BX + cc + 1]).then_inc(sca, 1)
                if i == 0:
                    act.wait_ge(rates_ready, 1)
                act.wait_ge(sca, 6 * i + 4)
                for c in range(2):
                    cc = 2 * i + c
                    nc.scalar.activation(a_dec[:, c], r_gate[:, c], ACT.Exp, scale=decay[:, 7, cc:cc + 1]).then_inc(sca, 1)
                    nc.scalar.activation(a_th[:, c], r_gate[:, c], ACT.Tanh, scale=decay[:, 6, cc:cc + 1])
                act.wait_ge(sca, 6 * i + 6)
                nc.scalar.activation(a_sq, a_dec, ACT.Square).then_inc(decays_ready, 1)
                act.wait_ge(square1_ready, i + 1)
                nc.scalar.activation(a_th, a_sq, ACT.Sqrt).then_inc(scale_ready, 1)

            lru_front(0)
            lru_front(1)
            act.wait_ge(centred, 1)
            nc.scalar.activation(square, conv, ACT.Square).then_inc(square_ready, 1)
            lru_front(2)
            act.wait_ge(cvar_ready, 1)
            nc.scalar.activation(conf_rstd, psum[:, 7, 0:SEQ], ACT.Sqrt, bias=eps[:, 0:1]).then_inc(conf_root, 1)
            act.wait_ge(conf_normed, 1)
            for c in range(CT):
                ins = nc.scalar.activation(mix_t[:, CT + c, :], conv[:, c], ACT.Silu, bias=chan[:, R_CLB + c:R_CLB + c + 1],
                                           scale=chan[:, R_CLG + c:R_CLG + c + 1])
            ins.then_inc(conf_done, 1)
            lru_front(3)

            for t in range(TT):
                act.wait_ge(var_ready, TT + t + 1)
                nc.scalar.activation(rstd[:, t:t + 1], moments[:, t, 1:2], ACT.Sqrt, bias=eps[:, 0:1]).then_inc(root_ready, 1)
            for f in range(0, 8, 2):
                act.wait_ge(h2_turned, f + 1)
                nc.scalar.copy(h_t[:, 4 * (f % 4):4 * (f % 4) + 4, (f // 4) * P:(f // 4 + 1) * P],
                               psum[:, 4 + f % 4, :].rearrange("p (a b) -> p a b", a=4)).then_inc(h2t_act, 1)
            act.wait_ge(exps_in, 1)
            nc.scalar.activation(rt[:, 480:490], rt[:, 470:480], ACT.Exp).then_inc(exps_ready, 1)

            def take_gather(p, i, parity):
                act.wait_ge(xg_gathered, p * GATHERS + i + 1)
                for b in range(2):
                    ins = nc.scalar.copy(xg[:, b * 8:(b + 1) * 8, :], psum[:, b, :].rearrange("p (k s) -> p k s", k=8))
                ins.then_inc(xg_copied, 1)
                act.wait_ge(q_turned, p * GATHERS + i + 1)
                nc.scalar.copy(place[:, parity, :], psum[:, 3, 0:SEQ]).then_inc(q_copied, 1)

            def experts_pass(p):
                take_gather(p, 0, 0)
                with act.Fori(0, LOOPS) as g:
                    for j in range(UNROLL):
                        e = g * UNROLL + j
                        n = p * EXPERTS + e
                        act.wait_ge(gu_used, (n + 1) * GU_PIECES)
                        nc.scalar.activation(sig, psum[:, 2, 0:F // 2], ACT.Silu).then_inc(silu_done, 1)
                        take_gather(p, e + 1, (j + 1) % 2)
                        act.wait_ge(hid_turned, n + 1)
                        nc.scalar.copy(hid_t, psum[:, 3, 0:2 * P].rearrange("p (c s) -> p c s", c=2)).then_inc(hid_copied, 1)
                        act.wait_ge(down_used, (n + 1) * DOWN_PIECES)
                        for b in range(2):
                            ins = nc.scalar.copy(y_sb[:, b], psum[:, 4 + b, :])
                        ins.then_inc(y_copied, 1)

            experts_pass(0)
            act.wait_ge(more_ready, 1)
            with act.Fori(1, PASSES) as p:
                needed = act.value_load(more[0:1, bass.ds(p, 1)], min_val=0, max_val=1)
                with act.If(needed > 0):
                    experts_pass(p)

            for t in range(TT):
                act.wait_ge(var_ready, 2 * TT + t + 1)
                nc.scalar.activation(rstd[:, t:t + 1], moments[:, t, 1:2], ACT.Sqrt, bias=eps[:, 0:1]).then_inc(root_ready, 1)

        @block.vector
        def _(dve):
            steps = [0]

            def step(ins):
                steps[0] += 1
                ins.then_inc(vec, 1)
                return steps[0]

            def link(ins):
                dve.wait_ge(vec, step(ins))

            V = nc.vector

            def moments_of(t, src, pieces, width):
                for i in range(pieces):
                    link(V.bn_stats(out=stats[:, t, i, :], in_=src[:, t, i * width:(i + 1) * width]))
                aggregate(t, pieces)

            def aggregate(t, pieces):
                V.bn_aggr(out=moments[:, t, :], in_=stats[:, t, 0:pieces, :].rearrange("p a b -> p (a b)")).then_inc(var_ready, 1)

            def standardise(t, n, src):
                dve.wait_ge(root_ready, n)
                link(V.reciprocal(rstd[:, t:t + 1], rstd[:, t:t + 1]))
                return V.tensor_scalar(out=src[:, t, :], in0=src[:, t, :], scalar1=moments[:, t, 0:1],
                                       scalar2=rstd[:, t:t + 1], op0=ALU.subtract, op1=ALU.mult)

            for t in range(TT):
                dve.wait_ge(x_here[t], 16)
                moments_of(t, rows, 4, 512)
            for t in range(TT):
                standardise(t, t + 1, rows).then_inc(norm_ready, 1)
            dve.wait_ge(chan_ready, 1)
            for f in range(1, 8, 2):
                dve.wait_ge(h_turned, f + 1)
                for k in range(4):
                    kk = 4 * (f % 4) + k
                    ins = V.tensor_scalar(out=h_t[:, kk, (f // 4) * P:(f // 4 + 1) * P], in0=psum[:, 4 + f % 4, k * P:(k + 1) * P],
                                          scalar1=chan[:, R_LNG + kk:R_LNG + kk + 1], scalar2=chan[:, R_LNB + kk:R_LNB + kk + 1],
                                          op0=ALU.mult, op1=ALU.add)
                ins.then_inc(ht_vec, 1)

            dve.wait_ge(gain_here[0], 32)
            dve.wait_ge(norm_ready, TT)
            for t in range(TT):
                m = step(V.tensor_tensor(rows[:, t, :], rows[:, t, :], gain, ALU.mult))
            dve.wait_ge(vec, m)
            for t in range(TT):
                ins = V.tensor_tensor(rows[:, t, :], rows[:, t, :], shift, ALU.add)
            ins.then_inc(gain_used, 1)

            lam = chan[:, R_LAM:R_LAM + CT]
            V.scalar_tensor_tensor(out=decay[:, 0, :], in0=lam, scalar=-1.0, in1=lam, op0=ALU.mult, op1=ALU.min).then_inc(rates_in, 1)
            dve.wait_ge(rates_exp, 1)
            link(V.tensor_scalar(out=decay[:, 2, :], in0=decay[:, 1, :], scalar1=2.0, scalar2=None, op0=ALU.add))
            link(V.reciprocal(decay[:, 2, :], decay[:, 2, :]))
            link(V.tensor_tensor(decay[:, 2, :], decay[:, 2, :], decay[:, 1, :], ALU.mult))
            link(V.tensor_tensor(decay[:, 3, :], decay[:, 2, :], decay[:, 2, :], ALU.mult))
            link(V.tensor_scalar(out=decay[:, 4, :], in0=decay[:, 3, :], scalar1=1.0 / 17, scalar2=None, op0=ALU.mult))
            for n in range(15, 1, -2):
                link(V.scalar_tensor_tensor(out=decay[:, 4, :], in0=decay[:, 4, :], scalar=1.0 / n, in1=decay[:, 3, :],
                                            op0=ALU.add, op1=ALU.mult))
            link(V.scalar_tensor_tensor(out=decay[:, 4, :], in0=decay[:, 4, :], scalar=1.0, in1=decay[:, 2, :],
                                        op0=ALU.add, op1=ALU.mult))
            link(V.tensor_scalar(out=decay[:, 5, :], in0=lam, scalar1=-1.0, scalar2=0.0, op0=ALU.mult, op1=ALU.max))
            link(V.scalar_tensor_tensor(out=decay[:, 5, :], in0=decay[:, 4, :], scalar=2.0, in1=decay[:, 5, :],
                                        op0=ALU.mult, op1=ALU.add))
            V.tensor_scalar(out=decay[:, 6, :], in0=decay[:, 5, :], scalar1=LRU_C, scalar2=None, op0=ALU.mult)
            V.tensor_scalar(out=decay[:, 7, :], in0=decay[:, 5, :], scalar1=-LRU_C, scalar2=None, op0=ALU.mult).then_inc(rates_ready, 1)

            def taps(dst, src, w_row, b_row, n, i):
                for k in range(n):
                    for c in range(2):
                        cc = 2 * i + c
                        w = chan[:, w_row + k * CT + cc:w_row + k * CT + cc + 1]
                        if k == 0:
                            m = step(V.tensor_scalar(out=dst[c], in0=src[:, c, 0:SEQ], scalar1=w,
                                                     scalar2=chan[:, b_row + cc:b_row + cc + 1], op0=ALU.mult, op1=ALU.add))
                        else:
                            dve.wait_ge(vec, m - 1)
                            m = step(V.scalar_tensor_tensor(out=dst[c], in0=src[:, c, k:k + SEQ], scalar=w, in1=dst[c],
                                                            op0=ALU.mult, op1=ALU.add))
                return m

            dve.wait_ge(consts, 2)
            for i in range(PAIRS):
                dve.wait_ge(conf_sig_ready, i + 1)
                V.tensor_tensor(glu[:, i % 2, :, CONF_TAPS - 1:], conf_sig, psum[:, (2 * i) % 4, :].rearrange(
                    "p (a b) -> p a b", a=2), ALU.mult).then_inc(glu_ready, 1)
                dve.wait_ge(glu_ready, i + 1)
                m = taps([conv[:, 2 * i + c] for c in range(2)], glu[:, i % 2], R_CCW, R_CCB, CONF_TAPS, i)
            dve.wait_ge(vec, m)

            def lru_conv(i):
                dve.wait_ge(lru_in_ready, i + 1)
                b = i % 2
                m = taps([a_in[:, b, c] for c in range(2)], lru_in[:, b], R_LCW, R_LCB, LRU_TAPS - 1, i)
                for c in range(2):
                    cc = 2 * i + c
                    k = LRU_TAPS - 1
                    dve.wait_ge(vec, m - 1 + c)
                    ins = V.scalar_tensor_tensor(out=a_in[:, b, c], in0=lru_in[:, b, c, k:k + SEQ],
                                                 scalar=chan[:, R_LCW + k * CT + cc:R_LCW + k * CT + cc + 1],
                                                 in1=a_in[:, b, c], op0=ALU.mult, op1=ALU.add)
                ins.then_inc(a_in_ready, 1)

            def lru_back(i):
                b = i % 2
                dve.wait_ge(decays_ready, i + 1)
                dve.wait_ge(a_in_ready, i + 1)
                V.scalar_tensor_tensor(out=a_sq, in0=a_sq, scalar=1.0, in1=a_th, op0=ALU.add, op1=ALU.mult).then_inc(square1_ready, 1)
                link(V.tensor_tensor(drive, i_gate, a_in[:, b], ALU.mult))
                dve.wait_ge(scale_ready, i + 1)
                link(V.tensor_tensor(drive, drive, a_th, ALU.mult))
                for c in range(2):
                    m = step(V.tensor_tensor_scan(out=state[:, c], data0=a_dec[:, c], data1=drive[:, c], initial=0.0,
                                                  op0=ALU.mult, op1=ALU.add))
                dve.wait_ge(vec, m)
                dve.wait_ge(gelu_ready, i + 1)
                V.tensor_tensor(mix_t[:, 2 * i:2 * i + 2, :], state, gelu[:, b], ALU.mult).then_inc(lru_done, 1)

            V.tensor_copy(decay[:, 0, 0:1], conv[:, CT - 1, 0:1]).then_inc(conv_ready, 1)
            lru_conv(0)
            lru_back(0)
            lru_conv(1)
            lru_back(1)
            dve.wait_ge(mean_ready, 1)
            for c in range(CT):
                ins = V.tensor_tensor(conv[:, c], conv[:, c], psum[:, 6, 0:SEQ], ALU.subtract)
            ins.then_inc(centred, 1)
            lru_conv(2)
            lru_back(2)
            dve.wait_ge(conf_root, 1)
            dve.wait_ge(centred, 1)
            link(V.reciprocal(conf_rstd, conf_rstd))
            for c in range(CT):
                ins = V.tensor_tensor(conv[:, c], conv[:, c], conf_rstd, ALU.mult)
            ins.then_inc(conf_normed, 1)
            lru_conv(3)
            lru_back(3)

            for n in range(OUT_CHUNKS):
                cols = slice(n * CHUNK, (n + 1) * CHUNK)
                dve.wait_ge(out_ready, n + 1)
                V.scalar_tensor_tensor(out=rows[:, :, cols], in0=rows[:, :, cols], scalar=ALPHA,
                                       in1=psum[:, n % 4, :].rearrange("p (a b) -> p a b", a=2),
                                       op0=ALU.mult, op1=ALU.add).then_inc(out_taken, 1)
                dve.wait_ge(out_taken, n + 1)
                for t in range(TT):
                    m = step(V.bn_stats(out=stats[:, t, n, :], in_=rows[:, t, cols]))
            dve.wait_ge(vec, m)
            for t in range(TT):
                aggregate(t, 8)
            dve.wait_ge(gain_here[1], 32)
            for t in range(TT):
                link(standardise(t, TT + t + 1, rows))
                link(V.tensor_tensor(rows[:, t, :], rows[:, t, :], gain, ALU.mult))
                V.tensor_tensor(rows[:, t, :], rows[:, t, :], shift, ALU.add).then_inc(h2_ready, 1)
            for f in range(1, 8, 2):
                dve.wait_ge(h2_turned, f + 1)
                V.tensor_copy(h_t[:, 4 * (f % 4):4 * (f % 4) + 4, (f // 4) * P:(f // 4 + 1) * P],
                              psum[:, 4 + f % 4, :].rearrange("p (a b) -> p a b", a=4)).then_inc(h2t_vec, 1)

            big = 1e30
            at = [EXPERTS]

            def small(*shape):
                n = 1
                for s in shape:
                    n *= s
                a = at[0]
                at[0] = a + n
                assert at[0] <= 470
                v = rt[:, a:a + n]
                if len(shape) == 2:
                    return v.rearrange("p (a b) -> p a b", a=shape[0])
                return v

            number = rt[:, 0:EXPERTS]
            logits = small(TT, GROUPS + EXPERTS)
            top_g = small(TT, 1)
            cand = small(TT, EXPERTS)
            first = small(TT, 1)
            group = small(TT, GROUPS)
            top1 = small(TT, 1)
            top2 = small(TT, 1)
            hot1 = small(TT, EXPERTS)
            exp_in = rt[:, 470:480].rearrange("p (a b) -> p a b", a=TT)
            exp_out = rt[:, 480:490].rearrange("p (a b) -> p a b", a=TT)
            prob = rt[:, 490:492].rearrange("p (a b) -> p a b", a=TT)
            q1 = rt[:, 492:494].rearrange("p (a b) -> p a b", a=TT)
            q2 = rt[:, 494:496].rearrange("p (a b) -> p a b", a=TT)
            le = logits[:, :, GROUPS:]

            def wide(v, n):
                return v.to_broadcast([P, TT, n])

            def pick_first(dst, src, top, n):
                link(V.tensor_tensor(dst, src, wide(top, n), ALU.is_equal))
                for t in range(TT):
                    m = step(V.scalar_tensor_tensor(out=cand[:, t, 0:n], in0=number[:, 0:n], scalar=-64.0, in1=dst[:, t],
                                                    op0=ALU.add, op1=ALU.mult))
                dve.wait_ge(vec, m)
                link(V.tensor_reduce(out=first, in_=cand[:, :, 0:n], axis=AX.X, op=ALU.min))
                link(V.tensor_tensor(dst, cand[:, :, 0:n], wide(first, n), ALU.is_equal))

            dve.wait_ge(gates_here, 16 * 8)
            dve.wait_ge(logits_ready, 1)
            link(V.tensor_tensor(logits, psum[:, 0, 0:TT * (GROUPS + EXPERTS)].rearrange("p (a b) -> p a b", a=TT),
                                 router_b[:, :].unsqueeze(1).to_broadcast([P, TT, GROUPS + EXPERTS]), ALU.add))
            link(V.tensor_reduce(out=top_g, in_=logits[:, :, 0:GROUPS], axis=AX.X, op=ALU.max))
            link(V.tensor_tensor(exp_in[:, :, 0:GROUPS], logits[:, :, 0:GROUPS], wide(top_g, GROUPS), ALU.subtract))
            pick_first(group, logits[:, :, 0:GROUPS], top_g, GROUPS)
            link(V.tensor_scalar(out=group, in0=group, scalar1=-1.0, scalar2=big, op0=ALU.add, op1=ALU.mult))
            for t in range(TT):
                m = step(V.tensor_tensor(le[:, t].rearrange("p (g e) -> p g e", g=GROUPS),
                                         le[:, t].rearrange("p (g e) -> p g e", g=GROUPS),
                                         group[:, t].unsqueeze(2).to_broadcast([P, GROUPS, PER_GROUP]), ALU.add))
            dve.wait_ge(vec, m)
            link(V.tensor_reduce(out=top1, in_=le, axis=AX.X, op=ALU.max))
            pick_first(hot1, le, top1, EXPERTS)
            link(V.scalar_tensor_tensor(out=le, in0=hot1, scalar=-2 * big, in1=le, op0=ALU.mult, op1=ALU.add))
            link(V.tensor_reduce(out=top2, in_=le, axis=AX.X, op=ALU.max))
            V.tensor_tensor(exp_in[:, :, GROUPS:], top2, top1, ALU.subtract).then_inc(exps_in, 1)
            pick_first(mask, le, top2, EXPERTS)
            dve.wait_ge(exps_ready, 1)
            link(V.tensor_reduce(out=prob, in_=exp_out[:, :, 0:GROUPS], axis=AX.X, op=ALU.add))
            link(V.reciprocal(prob, prob))
            link(V.tensor_scalar(out=q1, in0=exp_out[:, :, GROUPS:], scalar1=1.0, scalar2=None, op0=ALU.add))
            link(V.reciprocal(q1, q1))
            link(V.tensor_tensor(q2, q1, exp_out[:, :, GROUPS:], ALU.mult))
            link(V.tensor_tensor(q1, q1, prob, ALU.mult))
            link(V.tensor_tensor(q2, q2, prob, ALU.mult))
            link(V.memset(weight[:, :, EXPERTS:], 0.0))
            link(V.tensor_tensor(weight[:, :, 0:EXPERTS], hot1, wide(q1, EXPERTS), ALU.mult))
            link(V.tensor_tensor(cand, mask, wide(q2, EXPERTS), ALU.mult))
            link(V.tensor_tensor(weight[:, :, 0:EXPERTS], weight[:, :, 0:EXPERTS], cand, ALU.add))
            link(V.tensor_tensor(mask, mask, hot1, ALU.add))
            V.memset(rank[:, :, EXPERTS:], -1.0).then_inc(masks_ready, 1)
            dve.wait_ge(ranks_ready, 1)
            link(V.scalar_tensor_tensor(out=cand, in0=psum[:, 1, 0:TT * EXPERTS].rearrange("p (a b) -> p a b", a=TT),
                                        scalar=1.0, in1=mask, op0=ALU.add, op1=ALU.mult))
            link(V.tensor_scalar(out=rank[:, :, 0:EXPERTS], in0=cand, scalar1=-1.0, scalar2=None, op0=ALU.add))
            link(V.tensor_reduce(out=first[:, 0], in_=psum[:, 2, 0:EXPERTS], axis=AX.X, op=ALU.max))
            for p in range(PASSES):
                ins = V.tensor_scalar(out=more[0:1, p:p + 1], in0=first[0:1, 0], scalar1=float(SLOTS * p) + 0.5, scalar2=None,
                                      op0=ALU.is_gt)
            ins.then_inc(more_ready, 1)

            def one_hots(p, i, column):
                ts = [(out_, w) for out_, w in ((pick, False), (pick_w, True))]
                for out_, weighted in ts:
                    for t in range(TT):
                        kw = dict(scalar2=weight[:, t, column], op1=ALU.mult) if weighted else dict(scalar2=None)
                        ins = V.tensor_scalar(out=out_[:, t, :], in0=slot_id[:, 0:out_.shape[-1]],
                                              scalar1=rank[:, t, column], op0=ALU.is_equal, **kw)
                ins.then_inc(onehot_ready, 1)

            def add_round(p, i, r):
                t, half = r // 2, r % 2
                dve.wait_ge(scattered, p * SCATTERS + i * ROUNDS + r + 1)
                dst = total[:, t, :].rearrange("p (b h c) -> p b h c", b=2, h=2)[:, :, half, :]
                V.tensor_tensor(dst, dst, psum[:, 6:8, :], ALU.add).then_inc(added, 1)

            def experts_pass(p):
                V.memset(place[:, 1, :], 0.0)
                one_hots(p, 0, slice(0, 1))
                with dve.Fori(0, LOOPS) as g:
                    for j in range(UNROLL):
                        e = g * UNROLL + j
                        dve.wait_ge(q_turned, p * GATHERS + e + 1)
                        one_hots(p, e + 1, bass.ds(e + 1, 1))
                        for r in range(ROUNDS):
                            add_round(p, e, r)
                        dve.wait_ge(silu_done, p * EXPERTS + e + 1)
                        V.tensor_tensor(hid, sig, psum[:, 2, F // 2:F], ALU.mult).then_inc(hid_ready, 1)
                for r in range(ROUNDS):
                    add_round(p, EXPERTS, r)

            dve.wait_ge(vec, steps[0])
            experts_pass(0)
            with dve.Fori(1, PASSES) as p:
                needed = dve.value_load(more[0:1, bass.ds(p, 1)], min_val=0, max_val=1)
                with dve.If(needed > 0):
                    dve.wait_ge(q_turned, p * GATHERS)
                    V.tensor_scalar(out=rank[:, :, :], in0=rank[:, :, :], scalar1=-float(SLOTS), scalar2=None,
                                    op0=ALU.add).then_inc(masks_ready, 1)
                    dve.wait_ge(masks_ready, p + 1)
                    experts_pass(p)

            for t in range(TT):
                moments_of(t, total, 4, 512)
            dve.wait_ge(gain_here[2], 32)
            for t in range(TT):
                link(standardise(t, 2 * TT + t + 1, total))
                link(V.tensor_tensor(total[:, t, :], total[:, t, :], gain2, ALU.mult))
                V.tensor_tensor(total[:, t, :], total[:, t, :], shift2, ALU.add).then_inc(out_part, 1)

        @block.tensor
        def _(pe):
            def mm(dst, lhs, rhs, first, last):
                return nc.tensor.matmul(dst, lhs, rhs, start=first, stop=last)

            pe.wait_ge(consts, 1)
            pe.wait_ge(params_here, 16 * 12)
            nc.tensor.transpose(psum[:, 3, 0:ROWS_A], raw_a[0:ROWS_A, :], ident[0:ROWS_A, 0:ROWS_A])
            nc.tensor.transpose(psum[:, 3, ROWS_A:ROWS_A + P], raw_t[:, 0, :], ident[:, :])
            n = TAP_ROWS - P
            nc.tensor.transpose(psum[:, 3, ROWS_A + P:ROWS_A + TAP_ROWS], raw_t[0:n, 1, :], ident[0:n, 0:n]).then_inc(params_turned, 1)

            def turn_rows(ready, base, done):
                for f in range(8):
                    if f % 4 == 0:
                        pe.wait_ge(ready, base + f // 4 + 1)
                    if f >= 4:
                        if f % 2 == 0:
                            pe.wait_ge(ht_act if done is h_turned else h2t_act, (f - 4) // 2 + 1)
                        else:
                            pe.wait_ge(ht_vec if done is h_turned else h2t_vec, (f - 4) // 2 + 1)
                    for k in range(4):
                        kk = 4 * (f % 4) + k
                        ins = nc.tensor.transpose(psum[:, 4 + f % 4, k * P:(k + 1) * P],
                                                  rows[:, f // 4, kk * P:(kk + 1) * P], ident[:, :])
                    ins.then_inc(done, 1)

            turn_rows(norm_ready, 0, h_turned)
            pe.wait_ge(ht_act, 4)
            pe.wait_ge(ht_vec, 4)

            def project(i):
                s = i % MIX_RING
                pe.wait_ge(arrived[s], 16 * (i // MIX_RING + 1))
                j = i - 4
                if j >= 0:
                    if j < 2 * PAIRS:
                        pe.wait_ge(glu_ready, j // 2 + 1) if j % 2 == 0 else pe.wait_ge(conf_sig_ready, j // 2 + 1)
                    else:
                        pe.wait_ge(lru_in_ready if j % 2 == 0 else gelu_ready, (j - 2 * PAIRS) // 2 + 1)
                for c in range(2):
                    for k in range(KD):
                        ins = mm(psum[:, i % 4, c * SEQ:(c + 1) * SEQ], mix_slot[s][:, k, c * P:(c + 1) * P], h_t[:, k, :],
                                 k == 0, k == KD - 1)
                ins.then_inc(z_ready, 1)

            def lru_gates(i):
                pe.wait_ge(a_in_ready, i + 1)
                if i >= 1:
                    pe.wait_ge(decays_ready, i)
                for bank, w in ((4, w_a), (5, w_x)):
                    for c in range(2):
                        ins = mm(psum[:, bank, c * SEQ:(c + 1) * SEQ], w[:, 2 * i + c, :], a_in[:, i % 2, c], True, True)
                ins.then_inc(gates_ready, 1)

            for i in range(2 * PAIRS):
                project(i)
            pe.wait_ge(gates_here, 16 * 8)
            for i in range(PAIRS):
                project(2 * PAIRS + 2 * i)
                project(2 * PAIRS + 2 * i + 1)
                lru_gates(i)
                if i == 1:
                    pe.wait_ge(conv_ready, 1)
                    for c in range(CT):
                        ins = mm(psum[:, 6, 0:SEQ], mean_w[:, :], conv[:, c], c == 0, c == CT - 1)
                    ins.then_inc(mean_ready, 1)
                if i == 2:
                    pe.wait_ge(square_ready, 1)
                    for c in range(CT):
                        ins = mm(psum[:, 7, 0:SEQ], mean_w[:, :], square[:, c], c == 0, c == CT - 1)
                    ins.then_inc(cvar_ready, 1)

            pe.wait_ge(conf_done, 1)
            pe.wait_ge(lru_done, PAIRS)
            for n in range(OUT_CHUNKS):
                i = len(in_cols) + n
                s = i % MIX_RING
                pe.wait_ge(arrived[s], 16 * (i // MIX_RING + 1))
                if n >= 4:
                    pe.wait_ge(out_taken, n - 3)
                for t in range(TT):
                    for k in range(KD):
                        ins = mm(psum[:, n % 4, t * SEQ:(t + 1) * SEQ], mix_t[:, k, t * P:(t + 1) * P], mix_slot[s][:, k, :],
                                 k == 0, k == KD - 1)
                ins.then_inc(out_ready, 1)

            turn_rows(h2_ready, 0, h2_turned)
            pe.wait_ge(h2t_act, 4)
            pe.wait_ge(h2t_vec, 4)
            n = GROUPS + EXPERTS
            for t in range(TT):
                for k in range(KD):
                    ins = mm(psum[:, 0, t * n:(t + 1) * n], h_t[:, k, t * P:(t + 1) * P], router_w[:, k, :], k == 0, k == KD - 1)
            ins.then_inc(logits_ready, 1)
            pe.wait_ge(masks_ready, 1)
            mm(psum[:, 1, 0:EXPERTS], before[:, :], mask[:, 0], True, True)
            mm(psum[:, 1, EXPERTS:2 * EXPERTS], before[:, :], mask[:, 1], True, False)
            mm(psum[:, 1, EXPERTS:2 * EXPERTS], ones[:, :], mask[:, 0], False, True)
            mm(psum[:, 2, 0:EXPERTS], ones[:, :], mask[:, 0], True, False)
            mm(psum[:, 2, 0:EXPERTS], ones[:, :], mask[:, 1], False, True).then_inc(ranks_ready, 1)

            def gather(p, i):
                pe.wait_ge(onehot_ready, p * GATHERS + i + 1)
                if not (isinstance(p, int) and p == 0 and isinstance(i, int)):
                    pe.wait_ge(xg_copied, p * GATHERS + i)
                for k in range(KD):
                    for t in range(TT):
                        ins = mm(psum[:, k // 8, (k % 8) * SLOTS:(k % 8 + 1) * SLOTS], rows[:, t, k * P:(k + 1) * P],
                                 pick[:, t, :], t == 0, t == TT - 1)
                ins.then_inc(xg_gathered, 1)
                if not (isinstance(p, int) and p == 0 and isinstance(i, int)):
                    pe.wait_ge(q_copied, p * GATHERS + i)
                for t in range(TT):
                    ins = nc.tensor.transpose(psum[:, 3, t * P:(t + 1) * P], pick_w[:, t, :], ident[:, :])
                ins.then_inc(q_turned, 1)

            def scatter_round(p, i, r, parity):
                pe.wait_ge(added, p * SCATTERS + i * ROUNDS + r + 1)
                t, half = r // 2, r % 2
                for b in range(2):
                    ins = mm(psum[:, 6 + b, :], place[b * SLOTS:(b + 1) * SLOTS, parity, t * P:(t + 1) * P],
                             y_sb[b * SLOTS:(b + 1) * SLOTS, half, :], True, True)
                ins.then_inc(scattered, 1)

            def experts_pass(p):
                gather(p, 0)
                with pe.Fori(0, LOOPS) as g:
                    turn = (p * LOOPS + g) * TURNS
                    for j in range(UNROLL):
                        e = g * UNROLL + j
                        n = p * EXPERTS + e

                        def here(q):
                            i = j * PIECES + q
                            s = i % RING
                            base = 16 * MIX_USES if s < MIX_RING else 0
                            pe.wait_ge(arrived[s], turn * 32 + base + 32 * (i // RING + 1))
                            return s

                        pe.wait_ge(xg_copied, p * GATHERS + e + 1)
                        pe.wait_ge(y_copied, n + 1)
                        for q in range(GU_PIECES):
                            s = here(q)
                            for k in range(KP):
                                kk = q * KP + k
                                for b in range(2):
                                    ins = mm(psum[b * SLOTS:(b + 1) * SLOTS, 2, :], xg[:, kk, :],
                                             gu_slot[s][:, :, k, b * F // 2:(b + 1) * F // 2], kk == 0, kk == KD - 1)
                            ins.then_inc(gu_used, 1)
                            scatter_round(p, e, q, (j + 1) % 2)
                        gather(p, e + 1)
                        pe.wait_ge(hid_ready, n + 1)
                        pe.wait_ge(q_copied, p * GATHERS + e + 2)
                        for c in range(2):
                            ins = nc.tensor.transpose(psum[:, 3, c * P:(c + 1) * P], hid[:, c * P:(c + 1) * P], ident[:, :])
                        ins.then_inc(hid_turned, 1)
                        pe.wait_ge(hid_copied, n + 1)
                        for q in range(DOWN_PIECES):
                            s = here(GU_PIECES + q)
                            for c in range(2):
                                for i in range(2):
                                    for b in range(2):
                                        col = (2 * b + i) * 512
                                        ins = mm(psum[b * SLOTS:(b + 1) * SLOTS, 4 + i, :], hid_t[:, c, q * SLOTS:(q + 1) * SLOTS],
                                                 down_slot[s][:, c, col:col + 512], q == 0 and c == 0, q == 1 and c == 1)
                            ins.then_inc(down_used, 1)
                pe.wait_ge(y_copied, (p + 1) * EXPERTS + 1)
                for r in range(ROUNDS):
                    scatter_round(p, EXPERTS, r, 1)

            experts_pass(0)
            pe.wait_ge(more_ready, 1)
            with pe.Fori(1, PASSES) as p:
                needed = pe.value_load(more[0:1, bass.ds(p, 1)], min_val=0, max_val=1)
                with pe.If(needed > 0):
                    experts_pass(p)


INPUTS = ["x", "ln_in_g", "ln_in_b", "w_in", "lru_conv_w", "lru_conv_b", "lru_w_a", "lru_b_a", "lru_w_x", "lru_b_x",
          "lru_lambda", "conf_conv_w", "conf_conv_b", "conf_ln_g", "conf_ln_b", "w_out", "ln1_g", "ln1_b",
          "router_group_w", "router_group_b", "router_expert_w", "router_expert_b", "exp_w_gate", "exp_w_up",
          "exp_w_down", "ln2_g", "ln2_b"]


def kernel(**inputs):
    import numpy as np
    import concourse.bacc as bacc
    from concourse.bass_utils import run_bass_kernel_spmd

    nc = bacc.Bacc("TRN2", target_bir_lowering=False, num_devices=1)
    arrays, io = {}, {}
    for name in INPUTS:
        a = np.ascontiguousarray(inputs[name])
        arrays[f"in_{name}"] = a
        io[name] = nc.dram_tensor(f"in_{name}", a.shape, mybir.dt.from_np(a.dtype), kind="ExternalInput").ap()
    out = nc.dram_tensor("out_0", (1, SEQ, D), mybir.dt.float32, kind="ExternalOutput").ap()
    build(nc, io, out)
    r = run_bass_kernel_spmd(nc, [arrays], core_ids=[0])
    return r.results[0]["out_0"]
```

```python
from contextlib import ExitStack

import concourse.bass as bass
from concourse import mybir

D = 2048
SEQ = 256
P = 128
TT = SEQ // P
KD = D // P
HALF = D // 2
CT = HALF // P
LRU_TAPS = 4
CONF_TAPS = 31
HEAD = 64
GROUPS = 4
PER_GROUP = 8
EXPERTS = GROUPS * PER_GROUP
F = D // 4
SLOTS = 64
BLOCKS = SEQ // SLOTS
ITEMS = (2 * SEQ - 1) // (SLOTS + 1)
ALPHA = 2.0 ** 0.25
EPS = 1e-5
LRU_C = 8.0

RING = 8
SLOT = 4096
MIX_RING = 4
CHUNK = SLOT // KD
PAIRS = HALF // CHUNK
OUT_CHUNKS = D // CHUNK
MIX_USES = (4 * PAIRS + OUT_CHUNKS) // MIX_RING
GU_PIECES = 4
DOWN_PIECES = 2
KP = KD // GU_PIECES
PAIR = 2 * (GU_PIECES + DOWN_PIECES)
UNROLL = 2
BODY = UNROLL * PAIR
TURNS = BODY // RING
NPAIRS = EXPERTS // 2
LOOPS = NPAIRS // UNROLL
QUARTERS = 4
ROUNDS = 8
ITEM_SLOT = 2
LAST_SLOT = 0

R_LNG, R_LNB = 0, KD
R_LCW = 2 * KD
R_LCB = R_LCW + LRU_TAPS * CT
R_BA, R_BX, R_LAM = R_LCB + CT, R_LCB + 2 * CT, R_LCB + 3 * CT
R_CCB, R_CLG, R_CLB = R_LCB + 4 * CT, R_LCB + 5 * CT, R_LCB + 6 * CT
ROWS_A = R_LCB + 7 * CT
R_CCW = ROWS_A
TAP_ROWS = CONF_TAPS * CT


def build(nc, io, out):
    f32 = mybir.dt.float32
    i32 = mybir.dt.int32
    ALU = mybir.AluOpType
    ACT = mybir.ActivationFunctionType
    AX = mybir.AxisListType

    ctx = ExitStack()
    with ctx:
        def sb(name, shape, dt=f32):
            return ctx.enter_context(nc.sbuf_tensor(name, shape, dt))

        def sem(name):
            return ctx.enter_context(nc.semaphore(name))

        ring = sb("ring", [P, RING, SLOT])
        rows = sb("rows", [P, TT, D])
        turned = sb("turned", [P, KD * SEQ])
        region = sb("region", [P, KD * SEQ])
        scaling = sb("scaling", [P, 2 * D])
        ident = sb("ident", [P, P])
        mean_w = sb("mean_w", [P, P])
        before = sb("before", [P, P])
        ones = sb("ones", [P, P])
        slot_id = sb("slot_id", [P, BLOCKS, SLOTS])
        router_w = sb("router_w", [P, KD, GROUPS + EXPERTS])
        router_b = sb("router_b", [P, GROUPS + EXPERTS])
        eps = sb("eps", [P, 1])
        stats = sb("stats", [P, TT, 8, 6])
        moments = sb("moments", [P, TT, 2])
        rstd = sb("rstd", [P, TT])
        rank = sb("rank", [P, TT, EXPERTS])
        weight = sb("weight", [P, TT, EXPERTS])
        mask = sb("mask", [P, TT, EXPERTS])[:, :, :]
        items = sb("items", [1, 3, ITEMS], i32)
        item_no = sb("item_no", [1, ITEMS])
        flag_val = sb("flag_val", [1, 2, 3 * EXPERTS])
        flags = sb("flags", [1, 4, 3 * EXPERTS])
        rt = sb("rt", [P, 512])
        psum = ctx.enter_context(nc.psum_tensor("psum", [P, 8, 512], f32))

        h_t = turned[:, :].rearrange("p (k t) -> p k t", k=KD)
        mix_t = region[:, :].rearrange("p (k t) -> p k t", k=KD)
        total = region[:, :].rearrange("p (t d) -> p t d", t=TT)
        gain = scaling[:, 0:D]
        shift = scaling[:, D:2 * D]
        gain2 = ring[:, LAST_SLOT, 0:D]
        shift2 = ring[:, LAST_SLOT, D:2 * D]

        scratch = ring[:, MIX_RING:RING, :].rearrange("p s f -> p (s f)")
        used = [0]

        def tmp(*shape):
            n = 1
            for s in shape:
                n *= s
            a = used[0]
            used[0] = a + n
            assert used[0] <= (RING - MIX_RING) * SLOT
            v = scratch[:, a:a + n]
            if len(shape) == 2:
                return v.rearrange("p (a b) -> p a b", a=shape[0])
            if len(shape) == 3:
                return v.rearrange("p (a b c) -> p a b c", a=shape[0], b=shape[1])
            return v

        raw_a = tmp(P)
        raw_t = tmp(2, P)
        chan = tmp(ROWS_A + TAP_ROWS)
        decay = tmp(8, CT)
        w_a = tmp(CT, P)
        w_x = tmp(CT, P)
        glu = tmp(2, 2, SEQ + CONF_TAPS - 1)
        conf_sig = tmp(2, SEQ)
        conv = tmp(CT, SEQ)
        square = tmp(CT, SEQ)
        conf_rstd = tmp(SEQ)
        lru_in = tmp(2, 2, SEQ + LRU_TAPS - 1)
        a_in = tmp(2, 2, SEQ)
        gelu = tmp(2, 2, SEQ)
        r_gate, i_gate, a_dec, a_sq, a_th, drive, state = (tmp(2, SEQ) for _ in range(7))

        xg = turned[:, 0:KD * P].rearrange("p (k s) -> p k s", k=KD)
        pick = turned[:, 2048:2304].rearrange("p (t s) -> p t s", t=TT)
        pick_w = turned[:, 2304:2560].rearrange("p (t s) -> p t s", t=TT)
        place = turned[:, 2560:3072].rearrange("p (a t) -> p a t", a=2)
        sig = turned[:, 3072:3328]
        hid = turned[:, 3328:3840].rearrange("p (a f) -> p a f", a=2)
        y_sb = scaling[:, 0:2048].rearrange("p (n c) -> p n c", n=4)
        hid_t = scaling[:, 2048:2560].rearrange("p (a c s) -> p a c s", a=2, c=2)

        x_here = [sem(f"x_here{t}") for t in range(TT)]
        gain_used = sem("gain_used")
        params_here = sem("params_here")
        gates_here = sem("gates_here")
        gain_here = [sem(f"gain_here{i}") for i in range(3)]
        arrived = [sem(f"arrived{s}") for s in range(RING)]
        consts = sem("consts")
        zeroed = sem("zeroed")
        params_turned = sem("params_turned")
        chan_ready = sem("chan_ready")
        vec = sem("vec")
        sca = sem("sca")
        var_ready = sem("var_ready")
        root_ready = sem("root_ready")
        norm_ready = sem("norm_ready")
        h_turned = sem("h_turned")
        ht_act = sem("ht_act")
        ht_vec = sem("ht_vec")
        z_ready = sem("z_ready")
        conf_sig_ready = sem("conf_sig_ready")
        glu_ready = sem("glu_ready")
        conv_ready = sem("conv_ready")
        mean_ready = sem("mean_ready")
        centred = sem("centred")
        square_ready = sem("square_ready")
        cvar_ready = sem("cvar_ready")
        conf_root = sem("conf_root")
        conf_normed = sem("conf_normed")
        conf_done = sem("conf_done")
        rates_in = sem("rates_in")
        rates_exp = sem("rates_exp")
        rates_ready = sem("rates_ready")
        lru_in_ready = sem("lru_in_ready")
        gelu_ready = sem("gelu_ready")
        a_in_ready = sem("a_in_ready")
        gates_ready = sem("gates_ready")
        decays_ready = sem("decays_ready")
        square1_ready = sem("square1_ready")
        scale_ready = sem("scale_ready")
        lru_done = sem("lru_done")
        out_ready = sem("out_ready")
        out_taken = sem("out_taken")
        h2_ready = sem("h2_ready")
        h2_turned = sem("h2_turned")
        h2t_act = sem("h2t_act")
        h2t_vec = sem("h2t_vec")
        logits_ready = sem("logits_ready")
        exps_in = sem("exps_in")
        exps_ready = sem("exps_ready")
        masks_ready = sem("masks_ready")
        ranks_ready = sem("ranks_ready")
        items_ready = sem("items_ready")
        onehot_ready = sem("onehot_ready")
        xg_gathered = sem("xg_gathered")
        xg_copied = sem("xg_copied")
        place_turned = sem("place_turned")
        place_copied = sem("place_copied")
        gu_used = sem("gu_used")
        silu_done = sem("silu_done")
        hid_ready = sem("hid_ready")
        hid_turned = sem("hid_turned")
        hid_copied = sem("hid_copied")
        down_used = sem("down_used")
        y_done = sem("y_done")
        y_copied = sem("y_copied")
        scattered = sem("scattered")
        added = sem("added")
        total_ready = sem("total_ready")
        i_onehot = sem("i_onehot")
        i_gathered = sem("i_gathered")
        i_xg = sem("i_xg")
        i_turned = sem("i_turned")
        i_place = sem("i_place")
        i_gu = sem("i_gu")
        i_silu = sem("i_silu")
        i_hid = sem("i_hid")
        i_hid_turned = sem("i_hid_turned")
        i_hid_copied = sem("i_hid_copied")
        i_down = sem("i_down")
        i_y = sem("i_y")
        i_scattered = sem("i_scattered")
        i_added = sem("i_added")
        out_part = sem("out_part")
        stored = sem("stored")

        x_v = io["x"].rearrange("b (t p) d -> (b t) p d", p=P)
        out_v = out.rearrange("b (t p) d -> (b t) p d", p=P)
        w_in_v = io["w_in"].rearrange("l (k p) c -> (l p) k c", p=P)
        w_out_v = io["w_out"].rearrange("l (k p) c -> (l p) k c", p=P)
        w_gate_v = io["exp_w_gate"].rearrange("l g e (q k p) f -> (l g e) q p k f", p=P, k=KP)
        w_up_v = io["exp_w_up"].rearrange("l g e (q k p) f -> (l g e) q p k f", p=P, k=KP)
        w_down_v = io["exp_w_down"].rearrange("l g e (h c p) d -> (l g e) h c p d", p=P, c=2)
        gu_slot = [ring[:, s, :].rearrange("p (w k f) -> p w k f", w=2, k=KP) for s in range(RING)]
        down_slot = [ring[:, s, :].rearrange("p (c d) -> p c d", c=2) for s in range(RING)]
        mix_slot = [ring[:, s, :].rearrange("p (k c) -> p k c", k=KD) for s in range(MIX_RING)]

        in_cols = ([q * HALF + CHUNK * i for i in range(PAIRS) for q in (2, 3)]
                   + [q * HALF + CHUNK * i for i in range(PAIRS) for q in (0, 1)])

        block = ctx.enter_context(nc.Block())

        @block.sync
        def _(sp):
            for t in range(TT):
                sp.dma_start(rows[:, t, :], x_v[t]).then_inc(x_here[t], 16)
            for i, c in enumerate(in_cols):
                if i >= MIX_RING:
                    sp.wait_ge(z_ready, i - MIX_RING + 1)
                sp.dma_start(mix_slot[i % MIX_RING], w_in_v[:, :, c:c + CHUNK]).then_inc(arrived[i % MIX_RING], 16)
            for n in range(OUT_CHUNKS):
                i = len(in_cols) + n
                if n < MIX_RING:
                    sp.wait_ge(z_ready, i - MIX_RING + 1)
                else:
                    sp.wait_ge(out_ready, n - MIX_RING + 1)
                sp.dma_start(mix_slot[i % MIX_RING], w_out_v[:, :, n * CHUNK:(n + 1) * CHUNK]).then_inc(arrived[i % MIX_RING], 16)

            def load(s, q, expert, down):
                if not down:
                    for w, src in enumerate((w_gate_v, w_up_v)):
                        sp.dma_start(gu_slot[s][:, w], src[bass.ds(expert, 1), q].rearrange(
                            "o p k f -> (o p) k f")).then_inc(arrived[s], 16)
                else:
                    for c in range(2):
                        sp.dma_start(down_slot[s][:, c], w_down_v[bass.ds(expert, 1), q, c].rearrange(
                            "o p d -> (o p) d")).then_inc(arrived[s], 16)

            def await_piece(n, j):
                pair, q = n + j // PAIR, j % PAIR
                if q < 2 * GU_PIECES:
                    sp.wait_ge(gu_used, pair * 2 * GU_PIECES + q + 1)
                elif q < 2 * GU_PIECES + 2:
                    sp.wait_ge(down_used, pair + 1)
                else:
                    sp.wait_ge(y_done, pair * 4 + 4)

            def load_body(g):
                for j in range(BODY):
                    s = j % RING
                    if isinstance(g, int) and g == 0 and j < MIX_RING:
                        sp.wait_ge(out_ready, OUT_CHUNKS - MIX_RING + s + 1)
                    elif isinstance(g, int) and g == 0 and j < RING:
                        sp.wait_ge(lru_done, PAIRS)
                    else:
                        await_piece(g * UNROLL, j - RING)
                    first, q = 2 * (g * UNROLL + j // PAIR), j % PAIR
                    if q < 2 * GU_PIECES:
                        load(s, q % GU_PIECES, first + q // GU_PIECES, False)
                    else:
                        load(s, (q - 2 * GU_PIECES) // 2, first + q % 2, True)

            load_body(0)
            with sp.Fori(1, LOOPS) as g:
                load_body(g)
            await_piece((LOOPS - 1) * UNROLL, BODY - RING + LAST_SLOT)
            sp.dma_start(gain2, io["ln2_g"][0].partition_broadcast(P)).then_inc(gain_here[2], 16)
            sp.dma_start(shift2, io["ln2_b"][0].partition_broadcast(P)).then_inc(gain_here[2], 16)
            sp.wait_ge(y_done, NPAIRS * 4)
            sp.wait_ge(items_ready, 1)
            with sp.Fori(0, ITEMS) as i:
                needed = sp.value_load(items[0:1, 0, bass.ds(i, 1)], min_val=0, max_val=1)
                expert = sp.value_load(items[0:1, 1, bass.ds(i, 1)], min_val=0, max_val=EXPERTS - 1)
                with sp.If(needed > 0):
                    sp.wait_ge(i_down, i + 1)
                    for q in range(GU_PIECES):
                        load(ITEM_SLOT + q, q, expert, False)
                    for q in range(DOWN_PIECES):
                        load(ITEM_SLOT + GU_PIECES + q, q, expert, True)
            for t in range(TT):
                sp.wait_ge(out_part, t + 1)
                sp.dma_start(out_v[t], total[:, t, :]).then_inc(stored, 16)
            sp.wait_ge(stored, 16 * TT)

        @block.gpsimd
        def _(pool):
            nc.gpsimd.memset(ident[:, :], 0.0)
            nc.gpsimd.memset(before[:, :], 1.0).then_inc(zeroed, 1)
            pool.wait_ge(zeroed, 1)
            nc.gpsimd.affine_select(out=ident[:, :], in_=ident[:, :], compare_op=ALU.not_equal, fill=1.0,
                                    base=0, pattern=[[-1, P]], channel_multiplier=1)
            nc.gpsimd.affine_select(out=before[:, :], in_=before[:, :], compare_op=ALU.is_gt, fill=0.0,
                                    base=0, pattern=[[1, P]], channel_multiplier=-1)
            nc.gpsimd.memset(eps[:, :], EPS).then_inc(consts, 1)
            nc.gpsimd.memset(w_a, 0.0)
            nc.gpsimd.memset(w_x, 0.0).then_inc(zeroed, 1)
            nc.gpsimd.memset(glu[:, :, :, 0:CONF_TAPS - 1], 0.0)
            nc.gpsimd.memset(lru_in[:, :, :, 0:LRU_TAPS - 1], 0.0)
            nc.gpsimd.memset(ones[:, :], 1.0)
            nc.gpsimd.memset(mean_w[:, :], 1.0 / HALF)
            nc.gpsimd.iota(slot_id[:, :, :], pattern=[[1, SEQ]], base=0, channel_multiplier=0,
                           allow_small_or_imprecise_dtypes=True)
            nc.gpsimd.iota(item_no[:, :], pattern=[[1, ITEMS]], base=1, channel_multiplier=0,
                           allow_small_or_imprecise_dtypes=True)
            nc.gpsimd.iota(flag_val[:, 0, :], pattern=[[1, EXPERTS], [0, 3]], base=0, channel_multiplier=0,
                           allow_small_or_imprecise_dtypes=True)
            nc.gpsimd.iota(flag_val[:, 1, :], pattern=[[0, EXPERTS], [1, 3]], base=1, channel_multiplier=0,
                           allow_small_or_imprecise_dtypes=True)
            nc.gpsimd.iota(rt[:, 0:EXPERTS], pattern=[[1, EXPERTS]], base=0, channel_multiplier=0,
                           allow_small_or_imprecise_dtypes=True).then_inc(consts, 1)
            pool.wait_ge(gain_used, 1)
            pool.dma_start(gain, io["ln1_g"][0].partition_broadcast(P)).then_inc(gain_here[1], 16)
            pool.dma_start(shift, io["ln1_b"][0].partition_broadcast(P)).then_inc(gain_here[1], 16)
            for t in range(TT):
                pool.wait_ge(h2_ready, t + 1)
                ins = nc.gpsimd.tensor_scalar(out=total[:, t, :], in0=rows[:, t, :], scalar1=ALPHA, scalar2=0.0,
                                              op0=ALU.mult, op1=ALU.add)
            ins.then_inc(total_ready, 1)

        @block.scalar
        def _(act):
            def load_rows(name, r, n):
                src = io[name]
                src = src.rearrange("(c q) -> c q", q=P) if len(src.shape) == 1 else (
                    src.rearrange("l (c q) -> (l c) q", q=P) if len(src.shape) == 2 else
                    src.rearrange("l k (c q) -> (l k c) q", q=P))
                act.dma_start(raw_a[r:r + n, :], src).then_inc(params_here, 16)

            loaded = [("ln_in_g", R_LNG, KD), ("ln_in_b", R_LNB, KD), ("lru_conv_w", R_LCW, LRU_TAPS * CT),
                      ("lru_conv_b", R_LCB, CT), ("lru_b_a", R_BA, CT), ("lru_b_x", R_BX, CT),
                      ("lru_lambda", R_LAM, CT), ("conf_conv_b", R_CCB, CT), ("conf_ln_g", R_CLG, CT),
                      ("conf_ln_b", R_CLB, CT)]
            for name, r, n in loaded:
                load_rows(name, r, n)
            taps = io["conf_conv_w"].rearrange("l k (c q) -> (l k c) q", q=P)
            act.dma_start(raw_t[:, 0, :], taps[0:P]).then_inc(params_here, 16)
            act.dma_start(raw_t[0:TAP_ROWS - P, 1, :], taps[P:TAP_ROWS]).then_inc(params_here, 16)
            act.dma_start(gain, io["ln_in_g"].partition_broadcast(P)).then_inc(gain_here[0], 16)
            act.dma_start(shift, io["ln_in_b"].partition_broadcast(P)).then_inc(gain_here[0], 16)
            act.dma_start(router_w[:, :, 0:GROUPS], io["router_group_w"].rearrange("l (k p) g -> (l p) k g", p=P)).then_inc(gates_here, 16)
            act.dma_start(router_w[:, :, GROUPS:], io["router_expert_w"].rearrange("l (k p) g -> (l p) k g", p=P)).then_inc(gates_here, 16)
            act.dma_start(router_b[:, 0:GROUPS], io["router_group_b"][0].partition_broadcast(P)).then_inc(gates_here, 16)
            act.dma_start(router_b[:, GROUPS:], io["router_expert_b"][0].partition_broadcast(P)).then_inc(gates_here, 16)
            act.wait_ge(zeroed, 2)
            for dst, name in ((w_a, "lru_w_a"), (w_x, "lru_w_x")):
                for b in range(2):
                    src = io[name].rearrange("l (c b) i j -> (l b) i c j", b=2)[b]
                    act.dma_start(dst[b * HEAD:(b + 1) * HEAD, :, b * HEAD:(b + 1) * HEAD], src).then_inc(gates_here, 16)

            act.wait_ge(consts, 1)
            for t in range(TT):
                act.wait_ge(var_ready, t + 1)
                nc.scalar.activation(rstd[:, t:t + 1], moments[:, t, 1:2], ACT.Sqrt, bias=eps[:, 0:1]).then_inc(root_ready, 1)
            act.wait_ge(params_turned, 1)
            nc.scalar.copy(chan[:, 0:ROWS_A + TAP_ROWS], psum[:, 3, 0:ROWS_A + TAP_ROWS]).then_inc(chan_ready, 1)
            act.wait_ge(chan_ready, 1)
            for f in range(0, 2 * TT * 2, 2):
                act.wait_ge(h_turned, f + 1)
                for k in range(4):
                    kk = 4 * (f % 4) + k
                    ins = nc.scalar.activation(h_t[:, kk, (f // 4) * P:(f // 4 + 1) * P], psum[:, 4 + f % 4, k * P:(k + 1) * P],
                                               ACT.Identity, bias=chan[:, R_LNB + kk:R_LNB + kk + 1],
                                               scale=chan[:, R_LNG + kk:R_LNG + kk + 1])
                ins.then_inc(ht_act, 1)
            act.wait_ge(rates_in, 1)
            nc.scalar.activation(decay[:, 1, :], decay[:, 0, :], ACT.Exp).then_inc(rates_exp, 1)
            for i in range(PAIRS):
                act.wait_ge(z_ready, 2 * i + 2)
                if i >= 1:
                    act.wait_ge(glu_ready, i)
                nc.scalar.activation(conf_sig, psum[:, (2 * i + 1) % 4, :].rearrange("p (a b) -> p a b", a=2),
                                     ACT.Sigmoid).then_inc(conf_sig_ready, 1)

            def lru_front(i):
                b = i % 2
                act.wait_ge(z_ready, 2 * PAIRS + 2 * i + 1)
                if i >= 2:
                    act.wait_ge(a_in_ready, i - 1)
                nc.scalar.copy(lru_in[:, b, :, LRU_TAPS - 1:], psum[:, (2 * i) % 4, :].rearrange(
                    "p (a b) -> p a b", a=2)).then_inc(lru_in_ready, 1)
                act.wait_ge(z_ready, 2 * PAIRS + 2 * i + 2)
                if i >= 2:
                    act.wait_ge(lru_done, i - 1)
                nc.scalar.activation(gelu[:, b], psum[:, (2 * i + 1) % 4, :].rearrange("p (a b) -> p a b", a=2),
                                     ACT.Gelu_apprx_tanh).then_inc(gelu_ready, 1)
                act.wait_ge(gates_ready, i + 1)
                if i >= 1:
                    act.wait_ge(lru_done, i)
                for c in range(2):
                    cc = 2 * i + c
                    nc.scalar.activation(r_gate[:, c], psum[:, 4, c * SEQ:(c + 1) * SEQ], ACT.Sigmoid,
                                         bias=chan[:, R_BA + cc:R_BA + cc + 1]).then_inc(sca, 1)
                    nc.scalar.activation(i_gate[:, c], psum[:, 5, c * SEQ:(c + 1) * SEQ], ACT.Sigmoid,
                                         bias=chan[:, R_BX + cc:R_BX + cc + 1]).then_inc(sca, 1)
                if i == 0:
                    act.wait_ge(rates_ready, 1)
                act.wait_ge(sca, 6 * i + 4)
                for c in range(2):
                    cc = 2 * i + c
                    nc.scalar.activation(a_dec[:, c], r_gate[:, c], ACT.Exp, scale=decay[:, 7, cc:cc + 1]).then_inc(sca, 1)
                    nc.scalar.activation(a_th[:, c], r_gate[:, c], ACT.Tanh, scale=decay[:, 6, cc:cc + 1])
                act.wait_ge(sca, 6 * i + 6)
                nc.scalar.activation(a_sq, a_dec, ACT.Square).then_inc(decays_ready, 1)
                act.wait_ge(square1_ready, i + 1)
                nc.scalar.activation(a_th, a_sq, ACT.Sqrt).then_inc(scale_ready, 1)

            lru_front(0)
            lru_front(1)
            act.wait_ge(centred, 1)
            nc.scalar.activation(square, conv, ACT.Square).then_inc(square_ready, 1)
            lru_front(2)
            act.wait_ge(cvar_ready, 1)
            nc.scalar.activation(conf_rstd, psum[:, 7, 0:SEQ], ACT.Sqrt, bias=eps[:, 0:1]).then_inc(conf_root, 1)
            act.wait_ge(conf_normed, 1)
            for c in range(CT):
                ins = nc.scalar.activation(mix_t[:, CT + c, :], conv[:, c], ACT.Silu, bias=chan[:, R_CLB + c:R_CLB + c + 1],
                                           scale=chan[:, R_CLG + c:R_CLG + c + 1])
            ins.then_inc(conf_done, 1)
            lru_front(3)

            for t in range(TT):
                act.wait_ge(var_ready, TT + t + 1)
                nc.scalar.activation(rstd[:, t:t + 1], moments[:, t, 1:2], ACT.Sqrt, bias=eps[:, 0:1]).then_inc(root_ready, 1)
            for f in range(0, 8, 2):
                act.wait_ge(h2_turned, f + 1)
                nc.scalar.copy(h_t[:, 4 * (f % 4):4 * (f % 4) + 4, (f // 4) * P:(f // 4 + 1) * P],
                               psum[:, 4 + f % 4, :].rearrange("p (a b) -> p a b", a=4)).then_inc(h2t_act, 1)
            act.wait_ge(exps_in, 1)
            nc.scalar.activation(rt[:, 480:490], rt[:, 470:480], ACT.Exp).then_inc(exps_ready, 1)

            def take_quarter(n, q):
                act.wait_ge(xg_gathered, n * QUARTERS + q + 1)
                nc.scalar.copy(xg[:, q * 4:(q + 1) * 4, :], psum[:, 0, :].rearrange(
                    "p (k s) -> p k s", k=4)).then_inc(xg_copied, 1)

            def take_place(n, parity):
                act.wait_ge(place_turned, n + 1)
                nc.scalar.copy(place[:, parity, :], psum[:, 2, 0:SEQ]).then_inc(place_copied, 1)

            def silu(n, e):
                act.wait_ge(gu_used, (n * 2 + e + 1) * GU_PIECES)
                nc.scalar.activation(sig, psum[:, 1, 0:F // 2], ACT.Silu).then_inc(silu_done, 1)

            def take_hid(n, e):
                act.wait_ge(hid_turned, n * 2 + e + 1)
                nc.scalar.copy(hid_t[:, e], psum[:, 2, 0:2 * P].rearrange("p (c s) -> p c s", c=2)).then_inc(hid_copied, 1)

            def body(g, last=False):
                for u in range(UNROLL):
                    n = g * UNROLL + u
                    more = not (last and u == UNROLL - 1)
                    silu(n, 0)
                    take_hid(n, 0)
                    silu(n, 1)
                    if more:
                        take_quarter(n + 1, 0)
                    take_hid(n, 1)
                    if more:
                        for q in range(1, QUARTERS):
                            take_quarter(n + 1, q)
                        take_place(n + 1, (u + 1) % 2)
                    for i in range(4):
                        act.wait_ge(y_done, n * 4 + i + 1)
                        nc.scalar.copy(y_sb[:, i], psum[:, 4 + i, :]).then_inc(y_copied, 1)

            for q in range(QUARTERS):
                take_quarter(0, q)
            take_place(0, 0)
            with act.Fori(0, LOOPS - 1) as g:
                body(g)
            body(LOOPS - 1, last=True)

            act.wait_ge(items_ready, 1)
            with act.Fori(0, ITEMS) as i:
                needed = act.value_load(items[0:1, 0, bass.ds(i, 1)], min_val=0, max_val=1)
                with act.If(needed > 0):
                    act.wait_ge(i_gathered, i + 1)
                    for b in range(2):
                        ins = nc.scalar.copy(xg[:, b * 8:(b + 1) * 8, 0:SLOTS], psum[:, b, :].rearrange("p (k s) -> p k s", k=8))
                    ins.then_inc(i_xg, 1)
                    act.wait_ge(i_turned, i + 1)
                    nc.scalar.copy(place[:, 0, :], psum[:, 3, 0:SEQ]).then_inc(i_place, 1)
                    act.wait_ge(i_gu, i + 1)
                    nc.scalar.activation(sig, psum[:, 2, 0:F // 2], ACT.Silu).then_inc(i_silu, 1)
                    act.wait_ge(i_hid_turned, i + 1)
                    nc.scalar.copy(hid_t[:, 0], psum[:, 3, 0:2 * P].rearrange("p (c s) -> p c s", c=2)).then_inc(i_hid_copied, 1)
                    act.wait_ge(i_down, i + 2)
                    for b in range(2):
                        ins = nc.scalar.copy(y_sb[:, b], psum[:, 4 + b, :])
                    ins.then_inc(i_y, 1)

            for t in range(TT):
                act.wait_ge(var_ready, 2 * TT + t + 1)
                nc.scalar.activation(rstd[:, t:t + 1], moments[:, t, 1:2], ACT.Sqrt, bias=eps[:, 0:1]).then_inc(root_ready, 1)

        @block.vector
        def _(dve):
            steps = [0]

            def step(ins):
                steps[0] += 1
                ins.then_inc(vec, 1)
                return steps[0]

            def link(ins):
                dve.wait_ge(vec, step(ins))

            V = nc.vector

            def moments_of(t, src, pieces, width):
                for i in range(pieces):
                    link(V.bn_stats(out=stats[:, t, i, :], in_=src[:, t, i * width:(i + 1) * width]))
                aggregate(t, pieces)

            def aggregate(t, pieces):
                V.bn_aggr(out=moments[:, t, :], in_=stats[:, t, 0:pieces, :].rearrange("p a b -> p (a b)")).then_inc(var_ready, 1)

            def standardise(t, n, src):
                dve.wait_ge(root_ready, n)
                link(V.reciprocal(rstd[:, t:t + 1], rstd[:, t:t + 1]))
                return V.tensor_scalar(out=src[:, t, :], in0=src[:, t, :], scalar1=moments[:, t, 0:1],
                                       scalar2=rstd[:, t:t + 1], op0=ALU.subtract, op1=ALU.mult)

            for t in range(TT):
                dve.wait_ge(x_here[t], 16)
                moments_of(t, rows, 4, 512)
            for t in range(TT):
                standardise(t, t + 1, rows).then_inc(norm_ready, 1)
            dve.wait_ge(chan_ready, 1)
            for f in range(1, 8, 2):
                dve.wait_ge(h_turned, f + 1)
                for k in range(4):
                    kk = 4 * (f % 4) + k
                    ins = V.tensor_scalar(out=h_t[:, kk, (f // 4) * P:(f // 4 + 1) * P], in0=psum[:, 4 + f % 4, k * P:(k + 1) * P],
                                          scalar1=chan[:, R_LNG + kk:R_LNG + kk + 1], scalar2=chan[:, R_LNB + kk:R_LNB + kk + 1],
                                          op0=ALU.mult, op1=ALU.add)
                ins.then_inc(ht_vec, 1)

            dve.wait_ge(gain_here[0], 32)
            dve.wait_ge(norm_ready, TT)
            for t in range(TT):
                m = step(V.tensor_tensor(rows[:, t, :], rows[:, t, :], gain, ALU.mult))
            dve.wait_ge(vec, m)
            for t in range(TT):
                ins = V.tensor_tensor(rows[:, t, :], rows[:, t, :], shift, ALU.add)
            ins.then_inc(gain_used, 1)

            lam = chan[:, R_LAM:R_LAM + CT]
            V.scalar_tensor_tensor(out=decay[:, 0, :], in0=lam, scalar=-1.0, in1=lam, op0=ALU.mult, op1=ALU.min).then_inc(rates_in, 1)
            dve.wait_ge(rates_exp, 1)
            link(V.tensor_scalar(out=decay[:, 2, :], in0=decay[:, 1, :], scalar1=2.0, scalar2=None, op0=ALU.add))
            link(V.reciprocal(decay[:, 2, :], decay[:, 2, :]))
            link(V.tensor_tensor(decay[:, 2, :], decay[:, 2, :], decay[:, 1, :], ALU.mult))
            link(V.tensor_tensor(decay[:, 3, :], decay[:, 2, :], decay[:, 2, :], ALU.mult))
            link(V.tensor_scalar(out=decay[:, 4, :], in0=decay[:, 3, :], scalar1=1.0 / 17, scalar2=None, op0=ALU.mult))
            for n in range(15, 1, -2):
                link(V.scalar_tensor_tensor(out=decay[:, 4, :], in0=decay[:, 4, :], scalar=1.0 / n, in1=decay[:, 3, :],
                                            op0=ALU.add, op1=ALU.mult))
            link(V.scalar_tensor_tensor(out=decay[:, 4, :], in0=decay[:, 4, :], scalar=1.0, in1=decay[:, 2, :],
                                        op0=ALU.add, op1=ALU.mult))
            link(V.tensor_scalar(out=decay[:, 5, :], in0=lam, scalar1=-1.0, scalar2=0.0, op0=ALU.mult, op1=ALU.max))
            link(V.scalar_tensor_tensor(out=decay[:, 5, :], in0=decay[:, 4, :], scalar=2.0, in1=decay[:, 5, :],
                                        op0=ALU.mult, op1=ALU.add))
            V.tensor_scalar(out=decay[:, 6, :], in0=decay[:, 5, :], scalar1=LRU_C, scalar2=None, op0=ALU.mult)
            V.tensor_scalar(out=decay[:, 7, :], in0=decay[:, 5, :], scalar1=-LRU_C, scalar2=None, op0=ALU.mult).then_inc(rates_ready, 1)

            def taps(dst, src, w_row, b_row, n, i):
                for k in range(n):
                    for c in range(2):
                        cc = 2 * i + c
                        w = chan[:, w_row + k * CT + cc:w_row + k * CT + cc + 1]
                        if k == 0:
                            m = step(V.tensor_scalar(out=dst[c], in0=src[:, c, 0:SEQ], scalar1=w,
                                                     scalar2=chan[:, b_row + cc:b_row + cc + 1], op0=ALU.mult, op1=ALU.add))
                        else:
                            dve.wait_ge(vec, m - 1)
                            m = step(V.scalar_tensor_tensor(out=dst[c], in0=src[:, c, k:k + SEQ], scalar=w, in1=dst[c],
                                                            op0=ALU.mult, op1=ALU.add))
                return m

            dve.wait_ge(consts, 2)
            for i in range(PAIRS):
                dve.wait_ge(conf_sig_ready, i + 1)
                V.tensor_tensor(glu[:, i % 2, :, CONF_TAPS - 1:], conf_sig, psum[:, (2 * i) % 4, :].rearrange(
                    "p (a b) -> p a b", a=2), ALU.mult).then_inc(glu_ready, 1)
                dve.wait_ge(glu_ready, i + 1)
                m = taps([conv[:, 2 * i + c] for c in range(2)], glu[:, i % 2], R_CCW, R_CCB, CONF_TAPS, i)
            dve.wait_ge(vec, m)

            def lru_conv(i):
                dve.wait_ge(lru_in_ready, i + 1)
                b = i % 2
                m = taps([a_in[:, b, c] for c in range(2)], lru_in[:, b], R_LCW, R_LCB, LRU_TAPS - 1, i)
                for c in range(2):
                    cc = 2 * i + c
                    k = LRU_TAPS - 1
                    dve.wait_ge(vec, m - 1 + c)
                    ins = V.scalar_tensor_tensor(out=a_in[:, b, c], in0=lru_in[:, b, c, k:k + SEQ],
                                                 scalar=chan[:, R_LCW + k * CT + cc:R_LCW + k * CT + cc + 1],
                                                 in1=a_in[:, b, c], op0=ALU.mult, op1=ALU.add)
                ins.then_inc(a_in_ready, 1)

            def lru_back(i):
                b = i % 2
                dve.wait_ge(decays_ready, i + 1)
                dve.wait_ge(a_in_ready, i + 1)
                V.scalar_tensor_tensor(out=a_sq, in0=a_sq, scalar=1.0, in1=a_th, op0=ALU.add, op1=ALU.mult).then_inc(square1_ready, 1)
                link(V.tensor_tensor(drive, i_gate, a_in[:, b], ALU.mult))
                dve.wait_ge(scale_ready, i + 1)
                link(V.tensor_tensor(drive, drive, a_th, ALU.mult))
                for c in range(2):
                    m = step(V.tensor_tensor_scan(out=state[:, c], data0=a_dec[:, c], data1=drive[:, c], initial=0.0,
                                                  op0=ALU.mult, op1=ALU.add))
                dve.wait_ge(vec, m)
                dve.wait_ge(gelu_ready, i + 1)
                V.tensor_tensor(mix_t[:, 2 * i:2 * i + 2, :], state, gelu[:, b], ALU.mult).then_inc(lru_done, 1)

            V.tensor_copy(decay[:, 0, 0:1], conv[:, CT - 1, 0:1]).then_inc(conv_ready, 1)
            lru_conv(0)
            lru_back(0)
            lru_conv(1)
            lru_back(1)
            dve.wait_ge(mean_ready, 1)
            for c in range(CT):
                ins = V.tensor_tensor(conv[:, c], conv[:, c], psum[:, 6, 0:SEQ], ALU.subtract)
            ins.then_inc(centred, 1)
            lru_conv(2)
            lru_back(2)
            dve.wait_ge(conf_root, 1)
            dve.wait_ge(centred, 1)
            link(V.reciprocal(conf_rstd, conf_rstd))
            for c in range(CT):
                ins = V.tensor_tensor(conv[:, c], conv[:, c], conf_rstd, ALU.mult)
            ins.then_inc(conf_normed, 1)
            lru_conv(3)
            lru_back(3)

            for n in range(OUT_CHUNKS):
                cols = slice(n * CHUNK, (n + 1) * CHUNK)
                dve.wait_ge(out_ready, n + 1)
                V.scalar_tensor_tensor(out=rows[:, :, cols], in0=rows[:, :, cols], scalar=ALPHA,
                                       in1=psum[:, n % 4, :].rearrange("p (a b) -> p a b", a=2),
                                       op0=ALU.mult, op1=ALU.add).then_inc(out_taken, 1)
                dve.wait_ge(out_taken, n + 1)
                for t in range(TT):
                    m = step(V.bn_stats(out=stats[:, t, n, :], in_=rows[:, t, cols]))
            dve.wait_ge(vec, m)
            for t in range(TT):
                aggregate(t, 8)
            dve.wait_ge(gain_here[1], 32)
            for t in range(TT):
                link(standardise(t, TT + t + 1, rows))
                link(V.tensor_tensor(rows[:, t, :], rows[:, t, :], gain, ALU.mult))
                V.tensor_tensor(rows[:, t, :], rows[:, t, :], shift, ALU.add).then_inc(h2_ready, 1)
            for f in range(1, 8, 2):
                dve.wait_ge(h2_turned, f + 1)
                V.tensor_copy(h_t[:, 4 * (f % 4):4 * (f % 4) + 4, (f // 4) * P:(f // 4 + 1) * P],
                              psum[:, 4 + f % 4, :].rearrange("p (a b) -> p a b", a=4)).then_inc(h2t_vec, 1)

            big = 1e30
            at = [EXPERTS]

            def small(*shape):
                n = 1
                for s in shape:
                    n *= s
                a = at[0]
                at[0] = a + n
                assert at[0] <= 470
                v = rt[:, a:a + n]
                if len(shape) == 2:
                    return v.rearrange("p (a b) -> p a b", a=shape[0])
                return v

            number = rt[:, 0:EXPERTS]
            logits = small(TT, GROUPS + EXPERTS)
            top_g = small(TT, 1)
            cand = small(TT, EXPERTS)
            first = small(TT, 1)
            group = small(TT, GROUPS)
            top1 = small(TT, 1)
            top2 = small(TT, 1)
            hot1 = small(TT, EXPERTS)
            count = small(EXPERTS)[0:1]
            exp_in = rt[:, 470:480].rearrange("p (a b) -> p a b", a=TT)
            exp_out = rt[:, 480:490].rearrange("p (a b) -> p a b", a=TT)
            prob = rt[:, 490:492].rearrange("p (a b) -> p a b", a=TT)
            q1 = rt[:, 492:494].rearrange("p (a b) -> p a b", a=TT)
            q2 = rt[:, 494:496].rearrange("p (a b) -> p a b", a=TT)
            le = logits[:, :, GROUPS:]

            def wide(v, n):
                return v.to_broadcast([P, TT, n])

            def pick_first(dst, src, top, n):
                link(V.tensor_tensor(dst, src, wide(top, n), ALU.is_equal))
                for t in range(TT):
                    m = step(V.scalar_tensor_tensor(out=cand[:, t, 0:n], in0=number[:, 0:n], scalar=-64.0, in1=dst[:, t],
                                                    op0=ALU.add, op1=ALU.mult))
                dve.wait_ge(vec, m)
                link(V.tensor_reduce(out=first, in_=cand[:, :, 0:n], axis=AX.X, op=ALU.min))
                link(V.tensor_tensor(dst, cand[:, :, 0:n], wide(first, n), ALU.is_equal))

            dve.wait_ge(gates_here, 16 * 8)
            dve.wait_ge(logits_ready, 1)
            link(V.tensor_tensor(logits, psum[:, 0, 0:TT * (GROUPS + EXPERTS)].rearrange("p (a b) -> p a b", a=TT),
                                 router_b[:, :].unsqueeze(1).to_broadcast([P, TT, GROUPS + EXPERTS]), ALU.add))
            link(V.tensor_reduce(out=top_g, in_=logits[:, :, 0:GROUPS], axis=AX.X, op=ALU.max))
            link(V.tensor_tensor(exp_in[:, :, 0:GROUPS], logits[:, :, 0:GROUPS], wide(top_g, GROUPS), ALU.subtract))
            pick_first(group, logits[:, :, 0:GROUPS], top_g, GROUPS)
            link(V.tensor_scalar(out=group, in0=group, scalar1=-1.0, scalar2=big, op0=ALU.add, op1=ALU.mult))
            for t in range(TT):
                m = step(V.tensor_tensor(le[:, t].rearrange("p (g e) -> p g e", g=GROUPS),
                                         le[:, t].rearrange("p (g e) -> p g e", g=GROUPS),
                                         group[:, t].unsqueeze(2).to_broadcast([P, GROUPS, PER_GROUP]), ALU.add))
            dve.wait_ge(vec, m)
            link(V.tensor_reduce(out=top1, in_=le, axis=AX.X, op=ALU.max))
            pick_first(hot1, le, top1, EXPERTS)
            link(V.scalar_tensor_tensor(out=le, in0=hot1, scalar=-2 * big, in1=le, op0=ALU.mult, op1=ALU.add))
            link(V.tensor_reduce(out=top2, in_=le, axis=AX.X, op=ALU.max))
            V.tensor_tensor(exp_in[:, :, GROUPS:], top2, top1, ALU.subtract).then_inc(exps_in, 1)
            pick_first(mask, le, top2, EXPERTS)
            dve.wait_ge(exps_ready, 1)
            link(V.tensor_reduce(out=prob, in_=exp_out[:, :, 0:GROUPS], axis=AX.X, op=ALU.add))
            link(V.reciprocal(prob, prob))
            link(V.tensor_scalar(out=q1, in0=exp_out[:, :, GROUPS:], scalar1=1.0, scalar2=None, op0=ALU.add))
            link(V.reciprocal(q1, q1))
            link(V.tensor_tensor(q2, q1, exp_out[:, :, GROUPS:], ALU.mult))
            link(V.tensor_tensor(q1, q1, prob, ALU.mult))
            link(V.tensor_tensor(q2, q2, prob, ALU.mult))
            link(V.tensor_tensor(weight[:, :, 0:EXPERTS], hot1, wide(q1, EXPERTS), ALU.mult))
            link(V.tensor_tensor(cand, mask, wide(q2, EXPERTS), ALU.mult))
            link(V.tensor_tensor(weight[:, :, 0:EXPERTS], weight[:, :, 0:EXPERTS], cand, ALU.add))
            V.tensor_tensor(mask, mask, hot1, ALU.add).then_inc(masks_ready, 1)
            dve.wait_ge(ranks_ready, 1)
            link(V.scalar_tensor_tensor(out=cand, in0=psum[:, 1, 0:TT * EXPERTS].rearrange("p (a b) -> p a b", a=TT),
                                        scalar=1.0, in1=mask, op0=ALU.add, op1=ALU.mult))
            link(V.tensor_scalar(out=rank[:, :, 0:EXPERTS], in0=cand, scalar1=-1.0, scalar2=None, op0=ALU.add))
            link(V.tensor_copy(count, psum[0:1, 2, 0:EXPERTS]))

            def one_hot(t, e, column, block, s0, n):
                ids = slot_id[:, block, :]
                V.tensor_scalar(out=pick[:, t, s0:s0 + SLOTS], in0=ids, scalar1=rank[:, t, column], scalar2=None, op0=ALU.is_equal)
                for s in range(s0, s0 + n * SLOTS, SLOTS):
                    ins = V.tensor_scalar(out=pick_w[:, t, s:s + SLOTS], in0=ids, scalar1=rank[:, t, column],
                                          scalar2=weight[:, t, column], op0=ALU.is_equal, op1=ALU.mult)
                return ins

            def one_hots(n):
                for t in range(TT):
                    for e in range(2):
                        column = slice(e, e + 1) if isinstance(n, int) and n == 0 else bass.ds(2 * n + e, 1)
                        ins = one_hot(t, e, column, 0, e * SLOTS, 1)
                ins.then_inc(onehot_ready, 1)

            def add_round(n, r, bank=3):
                t, q = r // 4, r % 4
                dve.wait_ge(scattered, n * ROUNDS + r + 1)
                dst = total[:, t, q * 512:(q + 1) * 512]
                V.tensor_tensor(dst, dst, psum[:, bank, :], ALU.add).then_inc(added, 1)

            def hidden(n, e):
                dve.wait_ge(silu_done, n * 2 + e + 1)
                V.tensor_tensor(hid[:, e], sig, psum[:, 1, F // 2:F], ALU.mult).then_inc(hid_ready, 1)

            def body(g, first=False, last=False):
                for u in range(UNROLL):
                    n = g * UNROLL + u
                    adds = not (first and u == 0)
                    if not (last and u == UNROLL - 1):
                        dve.wait_ge(place_turned, n + 1)
                        one_hots(n + 1)
                    for e in range(2):
                        for r in range(4):
                            if r == 3:
                                hidden(n, e)
                            if adds:
                                add_round(n - 1, 4 * e + r)

            dve.wait_ge(vec, steps[0])
            one_hots(0)

            for b in range(1, BLOCKS):
                m = step(V.tensor_scalar(out=flags[:, 0, :].rearrange("p (e b) -> p e b", b=3)[:, :, b - 1:b],
                                         in0=count.unsqueeze(2), scalar1=SLOTS * b + 0.5, scalar2=None,
                                         op0=ALU.is_gt))
            dve.wait_ge(vec, m)
            link(V.tensor_tensor_scan(out=flags[:, 1, :], data0=ones[0:1, 0:3 * EXPERTS], data1=flags[:, 0, :], initial=0.0,
                                      op0=ALU.mult, op1=ALU.add))
            link(V.tensor_tensor(flags[:, 1, :], flags[:, 1, :], flags[:, 0, :], ALU.mult))
            for i in range(ITEMS):
                link(V.tensor_scalar(out=flags[:, 2, :], in0=flags[:, 1, :], scalar1=item_no[:, i:i + 1], scalar2=None,
                                     op0=ALU.is_equal))
                link(V.tensor_reduce(out=items[:, 0, i:i + 1], in_=flags[:, 2, :], axis=AX.X, op=ALU.max))
                for v in range(2):
                    link(V.tensor_tensor(flags[:, 3, :], flags[:, 2, :], flag_val[:, v, :], ALU.mult))
                    link(V.tensor_reduce(out=items[:, 1 + v, i:i + 1], in_=flags[:, 3, :], axis=AX.X, op=ALU.max))
            V.tensor_copy(items[:, 0, 0:1], items[:, 0, 0:1]).then_inc(items_ready, 1)

            dve.wait_ge(total_ready, 1)
            body(0, first=True)
            with dve.Fori(1, LOOPS - 1) as g:
                body(g)
            body(LOOPS - 1, last=True)
            for r in range(ROUNDS):
                add_round(NPAIRS - 1, r, bank=r % 4)

            with dve.Fori(0, ITEMS) as i:
                needed = dve.value_load(items[0:1, 0, bass.ds(i, 1)], min_val=0, max_val=1)
                expert = dve.value_load(items[0:1, 1, bass.ds(i, 1)], min_val=0, max_val=EXPERTS - 1)
                block_no = dve.value_load(items[0:1, 2, bass.ds(i, 1)], min_val=0, max_val=BLOCKS - 1)
                with dve.If(needed > 0):
                    for t in range(TT):
                        ids = slot_id[:, bass.ds(block_no, 1), :].rearrange("p o s -> p (o s)")
                        column = bass.ds(expert, 1)
                        V.tensor_scalar(out=pick[:, t, 0:SLOTS], in0=ids, scalar1=rank[:, t, column], scalar2=None, op0=ALU.is_equal)
                        for s in range(2):
                            ins = V.tensor_scalar(out=pick_w[:, t, s * SLOTS:(s + 1) * SLOTS], in0=ids, scalar1=rank[:, t, column],
                                                  scalar2=weight[:, t, column], op0=ALU.is_equal, op1=ALU.mult)
                    ins.then_inc(i_onehot, 1)
                    dve.wait_ge(i_silu, i + 1)
                    V.tensor_tensor(hid[:, 0], sig, psum[:, 2, F // 2:F], ALU.mult).then_inc(i_hid, 1)
                    for r in range(4):
                        t, half = r // 2, r % 2
                        dve.wait_ge(i_scattered, i * 4 + r + 1)
                        dst = total[:, t, :].rearrange("p (b h c) -> p b h c", b=2, h=2)[:, :, half, :]
                        V.tensor_tensor(dst, dst, psum[:, 6:8, :], ALU.add).then_inc(i_added, 1)

            for t in range(TT):
                moments_of(t, total, 4, 512)
            dve.wait_ge(gain_here[2], 32)
            for t in range(TT):
                link(standardise(t, 2 * TT + t + 1, total))
                link(V.tensor_tensor(total[:, t, :], total[:, t, :], gain2, ALU.mult))
                V.tensor_tensor(total[:, t, :], total[:, t, :], shift2, ALU.add).then_inc(out_part, 1)

        @block.tensor
        def _(pe):
            def mm(dst, lhs, rhs, first, last):
                return nc.tensor.matmul(dst, lhs, rhs, start=first, stop=last)

            pe.wait_ge(consts, 1)
            pe.wait_ge(params_here, 16 * 12)
            nc.tensor.transpose(psum[:, 3, 0:ROWS_A], raw_a[0:ROWS_A, :], ident[0:ROWS_A, 0:ROWS_A])
            nc.tensor.transpose(psum[:, 3, ROWS_A:ROWS_A + P], raw_t[:, 0, :], ident[:, :])
            n = TAP_ROWS - P
            nc.tensor.transpose(psum[:, 3, ROWS_A + P:ROWS_A + TAP_ROWS], raw_t[0:n, 1, :], ident[0:n, 0:n]).then_inc(params_turned, 1)

            def turn_rows(ready, base, done):
                for f in range(8):
                    if f % 4 == 0:
                        pe.wait_ge(ready, base + f // 4 + 1)
                    if f >= 4:
                        if f % 2 == 0:
                            pe.wait_ge(ht_act if done is h_turned else h2t_act, (f - 4) // 2 + 1)
                        else:
                            pe.wait_ge(ht_vec if done is h_turned else h2t_vec, (f - 4) // 2 + 1)
                    for k in range(4):
                        kk = 4 * (f % 4) + k
                        ins = nc.tensor.transpose(psum[:, 4 + f % 4, k * P:(k + 1) * P],
                                                  rows[:, f // 4, kk * P:(kk + 1) * P], ident[:, :])
                    ins.then_inc(done, 1)

            turn_rows(norm_ready, 0, h_turned)
            pe.wait_ge(ht_act, 4)
            pe.wait_ge(ht_vec, 4)

            def project(i):
                s = i % MIX_RING
                pe.wait_ge(arrived[s], 16 * (i // MIX_RING + 1))
                j = i - 4
                if j >= 0:
                    if j < 2 * PAIRS:
                        pe.wait_ge(glu_ready, j // 2 + 1) if j % 2 == 0 else pe.wait_ge(conf_sig_ready, j // 2 + 1)
                    else:
                        pe.wait_ge(lru_in_ready if j % 2 == 0 else gelu_ready, (j - 2 * PAIRS) // 2 + 1)
                for c in range(2):
                    for k in range(KD):
                        ins = mm(psum[:, i % 4, c * SEQ:(c + 1) * SEQ], mix_slot[s][:, k, c * P:(c + 1) * P], h_t[:, k, :],
                                 k == 0, k == KD - 1)
                ins.then_inc(z_ready, 1)

            def lru_gates(i):
                pe.wait_ge(a_in_ready, i + 1)
                if i >= 1:
                    pe.wait_ge(decays_ready, i)
                for bank, w in ((4, w_a), (5, w_x)):
                    for c in range(2):
                        ins = mm(psum[:, bank, c * SEQ:(c + 1) * SEQ], w[:, 2 * i + c, :], a_in[:, i % 2, c], True, True)
                ins.then_inc(gates_ready, 1)

            for i in range(2 * PAIRS):
                project(i)
            pe.wait_ge(gates_here, 16 * 8)
            for i in range(PAIRS):
                project(2 * PAIRS + 2 * i)
                project(2 * PAIRS + 2 * i + 1)
                lru_gates(i)
                if i == 1:
                    pe.wait_ge(conv_ready, 1)
                    for c in range(CT):
                        ins = mm(psum[:, 6, 0:SEQ], mean_w[:, :], conv[:, c], c == 0, c == CT - 1)
                    ins.then_inc(mean_ready, 1)
                if i == 2:
                    pe.wait_ge(square_ready, 1)
                    for c in range(CT):
                        ins = mm(psum[:, 7, 0:SEQ], mean_w[:, :], square[:, c], c == 0, c == CT - 1)
                    ins.then_inc(cvar_ready, 1)

            pe.wait_ge(conf_done, 1)
            pe.wait_ge(lru_done, PAIRS)
            for n in range(OUT_CHUNKS):
                i = len(in_cols) + n
                s = i % MIX_RING
                pe.wait_ge(arrived[s], 16 * (i // MIX_RING + 1))
                if n >= 4:
                    pe.wait_ge(out_taken, n - 3)
                for t in range(TT):
                    for k in range(KD):
                        ins = mm(psum[:, n % 4, t * SEQ:(t + 1) * SEQ], mix_t[:, k, t * P:(t + 1) * P], mix_slot[s][:, k, :],
                                 k == 0, k == KD - 1)
                ins.then_inc(out_ready, 1)

            turn_rows(h2_ready, 0, h2_turned)
            pe.wait_ge(h2t_act, 4)
            pe.wait_ge(h2t_vec, 4)
            n = GROUPS + EXPERTS
            for t in range(TT):
                for k in range(KD):
                    ins = mm(psum[:, 0, t * n:(t + 1) * n], h_t[:, k, t * P:(t + 1) * P], router_w[:, k, :], k == 0, k == KD - 1)
            ins.then_inc(logits_ready, 1)
            pe.wait_ge(masks_ready, 1)
            mm(psum[:, 1, 0:EXPERTS], before[:, :], mask[:, 0], True, True)
            mm(psum[:, 1, EXPERTS:2 * EXPERTS], before[:, :], mask[:, 1], True, False)
            mm(psum[:, 1, EXPERTS:2 * EXPERTS], ones[:, :], mask[:, 0], False, True)
            mm(psum[:, 2, 0:EXPERTS], ones[:, :], mask[:, 0], True, False)
            mm(psum[:, 2, 0:EXPERTS], ones[:, :], mask[:, 1], False, True).then_inc(ranks_ready, 1)

            def gather(n, q):
                if q == 0:
                    pe.wait_ge(onehot_ready, n + 1)
                if not (isinstance(n, int) and n == 0 and q == 0):
                    pe.wait_ge(xg_copied, n * QUARTERS + q)
                for k in range(4):
                    kk = 4 * q + k
                    for t in range(TT):
                        ins = mm(psum[:, 0, k * P:(k + 1) * P], rows[:, t, kk * P:(kk + 1) * P], pick[:, t, :], t == 0, t == TT - 1)
                ins.then_inc(xg_gathered, 1)

            def turn_place(n):
                for t in range(TT):
                    ins = nc.tensor.transpose(psum[:, 2, t * P:(t + 1) * P], pick_w[:, t, :], ident[:, :])
                ins.then_inc(place_turned, 1)

            def scatter_round(n, r, parity, bank=3):
                if r < 4:
                    pe.wait_ge(y_copied, n * 4 + r + 1)
                t, q = r // 4, r % 4
                mm(psum[:, bank, :], place[:, parity, t * P:(t + 1) * P], y_sb[:, q, :], True, True).then_inc(scattered, 1)

            def turn_hid(n, e):
                pe.wait_ge(hid_ready, n * 2 + e + 1)
                for c in range(2):
                    ins = nc.tensor.transpose(psum[:, 2, c * P:(c + 1) * P], hid[:, e, c * P:(c + 1) * P], ident[:, :])
                ins.then_inc(hid_turned, 1)

            def gate_up(slot, k, kk, bank, cols):
                for b in range(2):
                    ins = mm(psum[b * SLOTS:(b + 1) * SLOTS, bank, :], xg[:, kk, cols],
                             gu_slot[slot][:, :, k, b * F // 2:(b + 1) * F // 2], kk == 0, kk == KD - 1)
                return ins

            def body(g, first=False, last=False):
                for u in range(UNROLL):
                    n = g * UNROLL + u
                    scatters = not (first and u == 0)
                    more = not (last and u == UNROLL - 1)

                    def here(q):
                        j = u * PAIR + q
                        s = j % RING
                        pe.wait_ge(arrived[s], g * TURNS * 32 + (16 * MIX_USES if s < MIX_RING else 0) + 32 * (j // RING + 1))
                        return s

                    pe.wait_ge(xg_copied, (n + 1) * QUARTERS)
                    for e in range(2):
                        if e == 1:
                            pe.wait_ge(hid_ready, n * 2 + 1)
                        for q in range(GU_PIECES):
                            s = here(e * GU_PIECES + q)
                            for k in range(KP):
                                ins = gate_up(s, k, q * KP + k, 1, slice(e * SLOTS, (e + 1) * SLOTS))
                            ins.then_inc(gu_used, 1)
                            if scatters:
                                r = e * 4 + q
                                if not (isinstance(g, int) and n == 1 and r == 0):
                                    pe.wait_ge(added, (n - 1) * ROUNDS + r)
                                scatter_round(n - 1, r, (u + 1) % 2)
                            if e == 1 and q == 1:
                                pe.wait_ge(place_copied, n + 1)
                                turn_hid(n, 0)
                    if more:
                        gather(n + 1, 0)
                    pe.wait_ge(hid_copied, n * 2 + 1)
                    turn_hid(n, 1)
                    if more:
                        gather(n + 1, 1)
                    pe.wait_ge(hid_copied, n * 2 + 2)
                    for q in range(DOWN_PIECES):
                        s = [here(2 * GU_PIECES + 2 * q + e) for e in range(2)]

                        def down(c, i):
                            for e in range(2):
                                ins = mm(psum[e * SLOTS:(e + 1) * SLOTS, 4 + i, :], hid_t[:, e, c, q * SLOTS:(q + 1) * SLOTS],
                                         down_slot[s[e]][:, c, i * 512:(i + 1) * 512], q == 0 and c == 0, q == 1 and c == 1)
                            return ins

                        if q == 0:
                            for c in range(2):
                                for i in range(4):
                                    ins = down(c, i)
                                if c == 0 and more:
                                    gather(n + 1, 2)
                            ins.then_inc(down_used, 1)
                            if more:
                                gather(n + 1, 3)
                                turn_place(n + 1)
                        else:
                            for i in range(4):
                                down(0, i)
                                down(1, i).then_inc(y_done, 1)

            for q in range(QUARTERS):
                gather(0, q)
            turn_place(0)
            body(0, first=True)
            with pe.Fori(1, LOOPS - 1) as g:
                body(g)
            body(LOOPS - 1, last=True)
            for r in range(ROUNDS):
                if r == 3:
                    pe.wait_ge(added, (NPAIRS - 1) * ROUNDS)
                elif r > 3:
                    pe.wait_ge(added, (NPAIRS - 1) * ROUNDS + r - 3)
                scatter_round(NPAIRS - 1, r, (UNROLL - 1) % 2, bank=r % 4)

            pe.wait_ge(added, NPAIRS * ROUNDS)
            nc.tensor.transpose(psum[:, 3, 0:P], ident[:, :], ident[:, :]).then_inc(i_down, 1)
            pe.wait_ge(items_ready, 1)
            with pe.Fori(0, ITEMS) as i:
                needed = pe.value_load(items[0:1, 0, bass.ds(i, 1)], min_val=0, max_val=1)
                with pe.If(needed > 0):
                    pe.wait_ge(i_onehot, i + 1)
                    for k in range(KD):
                        for t in range(TT):
                            ins = mm(psum[:, k // 8, (k % 8) * SLOTS:(k % 8 + 1) * SLOTS], rows[:, t, k * P:(k + 1) * P],
                                     pick[:, t, 0:SLOTS], t == 0, t == TT - 1)
                    ins.then_inc(i_gathered, 1)
                    for t in range(TT):
                        ins = nc.tensor.transpose(psum[:, 3, t * P:(t + 1) * P], pick_w[:, t, :], ident[:, :])
                    ins.then_inc(i_turned, 1)

                    def item_here(q):
                        s = ITEM_SLOT + q
                        pe.wait_ge(arrived[s], i * 32 + 32 * LOOPS * TURNS + (16 * MIX_USES if s < MIX_RING else 0) + 32)
                        return s

                    pe.wait_ge(i_xg, i + 1)
                    for q in range(GU_PIECES):
                        s = item_here(q)
                        for k in range(KP):
                            ins = gate_up(s, k, q * KP + k, 2, slice(0, SLOTS))
                    ins.then_inc(i_gu, 1)
                    pe.wait_ge(i_hid, i + 1)
                    pe.wait_ge(i_place, i + 1)
                    for c in range(2):
                        ins = nc.tensor.transpose(psum[:, 3, c * P:(c + 1) * P], hid[:, 0, c * P:(c + 1) * P], ident[:, :])
                    ins.then_inc(i_hid_turned, 1)
                    pe.wait_ge(i_hid_copied, i + 1)
                    for q in range(DOWN_PIECES):
                        s = item_here(GU_PIECES + q)
                        for c in range(2):
                            for h in range(2):
                                for b in range(2):
                                    col = (2 * b + h) * 512
                                    ins = mm(psum[b * SLOTS:(b + 1) * SLOTS, 4 + h, :], hid_t[:, 0, c, q * SLOTS:(q + 1) * SLOTS],
                                             down_slot[s][:, c, col:col + 512], q == 0 and c == 0, q == 1 and c == 1)
                    ins.then_inc(i_down, 1)
                    pe.wait_ge(i_y, i + 1)
                    for r in range(4):
                        t, half = r // 2, r % 2
                        if r:
                            pe.wait_ge(i_added, i * 4 + r)
                        for b in range(2):
                            ins = mm(psum[:, 6 + b, :], place[b * SLOTS:(b + 1) * SLOTS, 0, t * P:(t + 1) * P],
                                     y_sb[b * SLOTS:(b + 1) * SLOTS, half, :], True, True)
                        ins.then_inc(i_scattered, 1)


INPUTS = ["x", "ln_in_g", "ln_in_b", "w_in", "lru_conv_w", "lru_conv_b", "lru_w_a", "lru_b_a", "lru_w_x", "lru_b_x",
          "lru_lambda", "conf_conv_w", "conf_conv_b", "conf_ln_g", "conf_ln_b", "w_out", "ln1_g", "ln1_b",
          "router_group_w", "router_group_b", "router_expert_w", "router_expert_b", "exp_w_gate", "exp_w_up",
          "exp_w_down", "ln2_g", "ln2_b"]


def kernel(**inputs):
    import numpy as np
    import concourse.bacc as bacc
    from concourse.bass_utils import run_bass_kernel_spmd

    nc = bacc.Bacc("TRN2", target_bir_lowering=False, num_devices=1)
    arrays, io = {}, {}
    for name in INPUTS:
        a = np.ascontiguousarray(inputs[name])
        arrays[f"in_{name}"] = a
        io[name] = nc.dram_tensor(f"in_{name}", a.shape, mybir.dt.from_np(a.dtype), kind="ExternalInput").ap()
    out = nc.dram_tensor("out_0", (1, SEQ, D), mybir.dt.float32, kind="ExternalOutput").ap()
    build(nc, io, out)
    r = run_bass_kernel_spmd(nc, [arrays], core_ids=[0])
    return r.results[0]["out_0"]
```

```python
from contextlib import ExitStack

import concourse.bass as bass
from concourse import mybir

D = 2048
SEQ = 256
P = 128
TT = SEQ // P
KD = D // P
HALF = D // 2
CT = HALF // P
LRU_TAPS = 4
CONF_TAPS = 31
HEAD = 64
GROUPS = 4
PER_GROUP = 8
EXPERTS = GROUPS * PER_GROUP
F = D // 4
SLOTS = 64
BLOCKS = SEQ // SLOTS
ITEMS = (2 * SEQ - 1) // (SLOTS + 1)
ALPHA = 2.0 ** 0.25
EPS = 1e-5
LRU_C = 8.0

RING = 8
SLOT = 4096
MIX_SLOTS = 4
RAW = 2
PART = SLOT // 2
CHUNK = SLOT // KD
PAIRS = HALF // CHUNK
OUT_CHUNKS = D // CHUNK
GU_PIECES = 4
DOWN_PIECES = 2
KP = KD // GU_PIECES
PAIR = 2 * (GU_PIECES + DOWN_PIECES)
UNROLL = 2
BODY = UNROLL * PAIR
TURNS = BODY // RING
NPAIRS = EXPERTS // 2
LOOPS = NPAIRS // UNROLL
QUARTERS = 4
ROUNDS = 8
END_BANKS = (3, 0, 2)
ITEM_BANKS = (3, 0, 1)
ITEM_PIECES = GU_PIECES + DOWN_PIECES
VEC_COLS = 896
LAST_SLOT = 6

N_G0, N_B0, N_G1, N_B1 = (i * KD for i in range(4))
ROWS_N = 4 * KD
R_LCW = 0
R_LCB = R_LCW + LRU_TAPS * CT
R_BA, R_BX, R_LAM = R_LCB + CT, R_LCB + 2 * CT, R_LCB + 3 * CT
R_CCB, R_CLG, R_CLB = R_LCB + 4 * CT, R_LCB + 5 * CT, R_LCB + 6 * CT
ROWS_A = R_LCB + 7 * CT
R_CCW = ROWS_A
TAP_ROWS = CONF_TAPS * CT

IN_ORDER = [("value", 0), ("gate", 0), ("value", 1), ("gate", 1), ("x", 0), ("g", 0), ("value", 2), ("gate", 2),
            ("value", 3), ("gate", 3), ("x", 1), ("g", 1), ("x", 2), ("x", 3), ("g", 2), ("g", 3)]
QUARTER_OF = {"x": 0, "g": 1, "value": 2, "gate": 3}


def build(nc, io, out):
    f32 = mybir.dt.float32
    f32r = mybir.dt.float32r
    i32 = mybir.dt.int32
    ALU = mybir.AluOpType
    ACT = mybir.ActivationFunctionType
    AX = mybir.AxisListType

    ctx = ExitStack()
    with ctx:
        def sb(name, shape, dt=f32):
            return ctx.enter_context(nc.sbuf_tensor(name, shape, dt))

        def sem(name):
            return ctx.enter_context(nc.semaphore(name))

        with ExitStack() as mixers:
            def early(name, shape, dt=f32):
                return mixers.enter_context(nc.sbuf_tensor(name, shape, dt))

            w_raw = early("w_raw", [P, RAW, SLOT])
            w_hi = early("w_hi", [P, 2, PART], f32r)
            w_lo = early("w_lo", [P, 2, PART], f32r)
            scratch = early("scratch", [P, (RING - MIX_SLOTS) * SLOT])
            act_hi = early("act_hi", [P, KD * SEQ], f32r)
            act_lo = early("act_lo", [P, KD * SEQ], f32r)
        ring = sb("ring", [P, RING, SLOT])
        turned = sb("turned", [P, KD * SEQ])
        scaling = sb("scaling", [P, 2 * D])
        region = sb("region", [P, KD * SEQ])
        rows = sb("rows", [P, TT, D])
        ident = sb("ident", [P, P])
        mean_w = sb("mean_w", [P, P])
        before = sb("before", [P, P])
        ones = sb("ones", [P, P])
        slot_id = sb("slot_id", [P, BLOCKS, SLOTS])
        router_w = sb("router_w", [P, KD, GROUPS + EXPERTS])
        router_b = sb("router_b", [P, GROUPS + EXPERTS])
        eps = sb("eps", [P, 1])
        stats = sb("stats", [P, TT, 8, 6])
        moments = sb("moments", [P, TT, 2])
        rstd = sb("rstd", [P, TT])
        offset = sb("offset", [P, 1])
        rank = sb("rank", [P, TT, EXPERTS])
        weight = sb("weight", [P, TT, EXPERTS])
        mask = sb("mask", [P, TT, EXPERTS])[:, :, :]
        items = sb("items", [1, 3, ITEMS + 1], i32)
        norm_p = sb("norm_p", [P, ROWS_N])
        raw_n = sb("raw_n", [ROWS_N, P])
        router_t = sb("router_t", [P, P])
        item_no = sb("item_no", [1, ITEMS + 1])
        flag_val = sb("flag_val", [1, 2, 3 * EXPERTS])
        flags = sb("flags", [1, 4, 3 * EXPERTS])
        rt = sb("rt", [P, 512])
        psum = ctx.enter_context(nc.psum_tensor("psum", [P, 8, 512], f32))

        h_t = turned[:, :].rearrange("p (k t) -> p k t", k=KD)
        mix_t = region[:, :].rearrange("p (k t) -> p k t", k=KD)
        total = region[:, :].rearrange("p (t d) -> p t d", t=TT)
        h_in_t = mix_t
        gain1 = region[:, 0:D]
        shift1 = region[:, D:2 * D]
        gain2 = ring[:, LAST_SLOT, 0:D]
        shift2 = ring[:, LAST_SLOT, D:2 * D]

        part_hi = act_hi[:, :].rearrange("p (k t) -> p k t", k=KD)
        part_lo = act_lo[:, :].rearrange("p (k t) -> p k t", k=KD)

        used = [0]

        def tmp(*shape):
            n = 1
            for s in shape:
                n *= s
            a = used[0]
            used[0] = a + n
            assert used[0] <= (RING - MIX_SLOTS) * SLOT
            v = scratch[:, a:a + n]
            if len(shape) == 2:
                return v.rearrange("p (a b) -> p a b", a=shape[0])
            if len(shape) == 3:
                return v.rearrange("p (a b c) -> p a b c", a=shape[0], b=shape[1])
            return v

        raw_a = tmp(P)
        raw_t = tmp(2, P)
        chan = tmp(ROWS_A + TAP_ROWS)
        decay = tmp(8, CT)
        w_a = tmp(CT, P)
        w_x = tmp(CT, P)
        glu = tmp(2, 2, SEQ + CONF_TAPS - 1)
        conf_sig = tmp(2, 2, SEQ)
        conv_flat = tmp(D)
        square_flat = tmp(D)
        conv = conv_flat.rearrange("p (c t) -> p c t", c=CT)
        square = square_flat.rearrange("p (c t) -> p c t", c=CT)
        gain0, shift0 = conv_flat, square_flat
        conf_rstd = tmp(SEQ)
        lru_in = tmp(2, 2, SEQ + LRU_TAPS - 1)
        a_in = tmp(2, 2, SEQ)
        gelu = tmp(2, 2, SEQ)
        r_gate, i_gate, a_dec, a_sq, a_th, drive, state = (tmp(2, SEQ) for _ in range(7))

        xg = turned[:, 0:KD * P].rearrange("p (k s) -> p k s", k=KD)
        pick = turned[:, 2048:2304].rearrange("p (t s) -> p t s", t=TT)
        pick_w = turned[:, 2304:2560].rearrange("p (t s) -> p t s", t=TT)
        place = turned[:, 2560:3072].rearrange("p (a t) -> p a t", a=2)
        sig = turned[:, 3072:3328]
        hid = turned[:, 3328:3840].rearrange("p (a f) -> p a f", a=2)
        y_sb = scaling[:, 0:2048].rearrange("p (n c) -> p n c", n=4)
        hid_t = scaling[:, 2048:2560].rearrange("p (a c s) -> p a c s", a=2, c=2)

        x_here = [sem(f"x_here{t}") for t in range(TT)]
        params_here = sem("params_here")
        gates_here = sem("gates_here")
        gain_here = [sem(f"gain_here{i}") for i in range(3)]
        chunk_here = [sem(f"chunk_here{s}") for s in range(RAW)]
        arrived = [sem(f"arrived{s}") for s in range(RING)]
        consts = sem("consts")
        zeroed = sem("zeroed")
        params_turned = sem("params_turned")
        chan_ready = sem("chan_ready")
        vec = sem("vec")
        sca = sem("sca")
        var_ready = sem("var_ready")
        root_ready = sem("root_ready")
        norm_ready = sem("norm_ready")
        norm_here = sem("norm_here")
        norm_turned = sem("norm_turned")
        norm_p_ready = sem("norm_p_ready")
        logits_t = sem("logits_t")
        logits_copied = sem("logits_copied")
        h_turned = sem("h_turned")
        ht_act = sem("ht_act")
        ht_vec = sem("ht_vec")
        hi_act = sem("hi_act")
        hi_vec = sem("hi_vec")
        h_lo_ready = sem("h_lo_ready")
        w_hi_ready = sem("w_hi_ready")
        w_lo_ready = sem("w_lo_ready")
        w_used = sem("w_used")
        tile_done = sem("tile_done")
        mix_hi = sem("mix_hi")
        mix_lo = sem("mix_lo")
        conf_sig_ready = sem("conf_sig_ready")
        glu_ready = sem("glu_ready")
        conv_ready = sem("conv_ready")
        mean_ready = sem("mean_ready")
        centred = sem("centred")
        square_ready = sem("square_ready")
        cvar_ready = sem("cvar_ready")
        conf_root = sem("conf_root")
        conf_normed = sem("conf_normed")
        conf_done = sem("conf_done")
        rates_in = sem("rates_in")
        rates_exp = sem("rates_exp")
        rates_ready = sem("rates_ready")
        lru_in_ready = sem("lru_in_ready")
        gelu_ready = sem("gelu_ready")
        a_in_ready = sem("a_in_ready")
        gates_ready = sem("gates_ready")
        decays_ready = sem("decays_ready")
        gap_ready = sem("gap_ready")
        scale_ready = sem("scale_ready")
        lru_done = sem("lru_done")
        state_ready = sem("state_ready")
        out_taken = sem("out_taken")
        h2_gained = sem("h2_gained")
        h2_ready = sem("h2_ready")
        h2_turned = sem("h2_turned")
        h2t_act = sem("h2t_act")
        h2t_vec = sem("h2t_vec")
        logits_ready = sem("logits_ready")
        exps_in = sem("exps_in")
        exps_ready = sem("exps_ready")
        masks_ready = sem("masks_ready")
        ranks_ready = sem("ranks_ready")
        items_ready = sem("items_ready")
        onehot_ready = sem("onehot_ready")
        xg_gathered = sem("xg_gathered")
        xg_copied = sem("xg_copied")
        place_turned = sem("place_turned")
        place_copied = sem("place_copied")
        gu_used = sem("gu_used")
        silu_done = sem("silu_done")
        hid_ready = sem("hid_ready")
        hid_turned = sem("hid_turned")
        hid_copied = sem("hid_copied")
        down_used = sem("down_used")
        y_done = sem("y_done")
        y_copied = sem("y_copied")
        scattered = sem("scattered")
        added = sem("added")
        total_ready = sem("total_ready")
        i_gu = sem("i_gu")
        i_silu = sem("i_silu")
        i_hid = sem("i_hid")
        i_hid_turned = sem("i_hid_turned")
        i_hid_copied = sem("i_hid_copied")
        i_down = sem("i_down")
        i_y = sem("i_y")
        i_scattered = sem("i_scattered")
        i_added = sem("i_added")
        stat_done = sem("stat_done")
        stats_seen = sem("stats_seen")
        gained = sem("gained")
        pool_gained = sem("pool_gained")
        rstd_ready = sem("rstd_ready")
        last_scaled = sem("last_scaled")
        pool_part = sem("pool_part")
        out_part = sem("out_part")
        stored = sem("stored")

        x_v = io["x"].rearrange("b (t p) d -> (b t) p d", p=P)
        out_v = out.rearrange("b (t p) d -> (b t) p d", p=P)
        w_in_v = io["w_in"].rearrange("l (k p) c -> (l p) k c", p=P)
        w_out_v = io["w_out"].rearrange("l (k p) c -> (l p) k c", p=P)
        w_gate_v = io["exp_w_gate"].rearrange("l g e (q k p) f -> (l g e) q p k f", p=P, k=KP)
        w_up_v = io["exp_w_up"].rearrange("l g e (q k p) f -> (l g e) q p k f", p=P, k=KP)
        w_down_v = io["exp_w_down"].rearrange("l g e (h c p) d -> (l g e) h c p d", p=P, c=2)
        gu_slot = [ring[:, s, :].rearrange("p (w k f) -> p w k f", w=2, k=KP) for s in range(RING)]
        down_slot = [ring[:, s, :].rearrange("p (c d) -> p c d", c=2) for s in range(RING)]
        raw_slot = [w_raw[:, s, :].rearrange("p (k c) -> p k c", k=KD) for s in range(RAW)]

        in_cols = [QUARTER_OF[q] * HALF + CHUNK * i for q, i in IN_ORDER]

        def chunk_no(q, i):
            return IN_ORDER.index((q, i))

        def chunk_bank(q, i):
            return psum[:, chunk_no(q, i) % 4, :].rearrange("p (a b) -> p a b", a=2)

        def bank_part(f):
            return slice(None), slice(4 * (f % 4), 4 * (f % 4) + 4), slice(f // 4 * P, (f // 4 + 1) * P)

        def raw_part(j):
            slot, b = raw_slot[j // 2 % RAW], j % 2
            return slot[:, :, b * P:(b + 1) * P] if j < 2 * len(IN_ORDER) else slot[:, b * CT:(b + 1) * CT, :]

        def split_part(w, j):
            return w[:, j % 2, :].rearrange("p (k c) -> p k c", k=KD if j < 2 * len(IN_ORDER) else CT)

        def gather_bank(n, q):
            return 4 + q if isinstance(n, int) and n == 0 else 0

        block = ctx.enter_context(nc.Block())

        @block.sync
        def _(sp):
            for t in range(TT):
                sp.dma_start(rows[:, t, :], x_v[t]).then_inc(x_here[t], 16)
            def load_chunk(i, src):
                if i >= RAW:
                    sp.wait_ge(w_lo_ready, 2 * (i - RAW) + 2)
                sp.dma_start(raw_slot[i % RAW], src).then_inc(chunk_here[i % RAW], 16)

            for i, c in enumerate(in_cols):
                if i == 1:
                    sp.wait_ge(params_here, 16 * 10)
                load_chunk(i, w_in_v[:, :, c:c + CHUNK])

            def load_gu(s, q, expert, w):
                src = (w_gate_v, w_up_v)[w]
                sp.dma_start(gu_slot[s][:, w], src[bass.ds(expert, 1), q].rearrange("o p k f -> (o p) k f")).then_inc(arrived[s], 16)

            early_halves = 2 * (RING - MIX_SLOTS)
            for n in range(OUT_CHUNKS):
                load_chunk(len(in_cols) + n, w_out_v[:, :, n * CHUNK:(n + 1) * CHUNK])
                if n == 2:
                    sp.wait_ge(lru_done, PAIRS)
                    sp.wait_ge(conf_done, 1)
                if n >= 2:
                    for half in range(n - 2, n - 1 if n < OUT_CHUNKS - 1 else early_halves):
                        load_gu(MIX_SLOTS + half // 2, half // 2, 1, half % 2)

            def load(s, q, expert, down):
                if not down:
                    for w in range(2):
                        load_gu(s, q, expert, w)
                else:
                    for c in range(2):
                        sp.dma_start(down_slot[s][:, c], w_down_v[bass.ds(expert, 1), q, c].rearrange(
                            "o p d -> (o p) d")).then_inc(arrived[s], 16)

            def await_piece(n, j):
                pair, q = n + j // PAIR, j % PAIR
                if q < 2 * GU_PIECES:
                    sp.wait_ge(gu_used, pair * 2 * GU_PIECES + q + 1)
                elif q < 2 * GU_PIECES + 2:
                    sp.wait_ge(down_used, pair + 1)
                else:
                    sp.wait_ge(y_done, pair * 4 + 4)

            def load_body(g):
                for j in range(BODY):
                    s = j % RING
                    if isinstance(g, int) and g == 0 and j < RAW:
                        sp.wait_ge(w_lo_ready, 2 * (len(in_cols) + OUT_CHUNKS - RAW + s) + 2)
                    elif isinstance(g, int) and g == 0 and j < MIX_SLOTS:
                        sp.wait_ge(w_used, 2 * (len(in_cols) + OUT_CHUNKS))
                    elif isinstance(g, int) and g == 0 and j < RING:
                        continue
                    else:
                        await_piece(g * UNROLL, j - RING)
                    first, q = 2 * (g * UNROLL + j // PAIR), j % PAIR
                    if q < 2 * GU_PIECES:
                        load(s, q % GU_PIECES, first + q // GU_PIECES, False)
                    else:
                        load(s, (q - 2 * GU_PIECES) // 2, first + q % 2, True)

            load_body(0)
            with sp.Fori(1, LOOPS) as g:
                load_body(g)

            def load_item(i):
                expert = sp.value_load(items[0:1, 1, bass.ds(i, 1)], min_val=0, max_val=EXPERTS - 1)
                for q in range(ITEM_PIECES):
                    if isinstance(i, int):
                        await_piece((LOOPS - 1) * UNROLL, BODY - RING + q)
                    elif q == 0:
                        sp.wait_ge(i_down, i * 4)
                    load(q, q % GU_PIECES, expert, q >= GU_PIECES)

            sp.wait_ge(items_ready, 1)
            n_items = sp.value_load(items[0:1, 0, 0:1], min_val=0, max_val=ITEMS)
            with sp.If(n_items > 0):
                load_item(0)
            await_piece((LOOPS - 1) * UNROLL, BODY - RING + LAST_SLOT)
            sp.dma_start(gain2, io["ln2_g"][0].partition_broadcast(P)).then_inc(gain_here[2], 16)
            sp.dma_start(shift2, io["ln2_b"][0].partition_broadcast(P)).then_inc(gain_here[2], 16)
            with sp.If(n_items > 1):
                with sp.Fori(1, ITEMS) as i:
                    with sp.If(n_items > i):
                        load_item(i)
            for t, cols, part, n in ((0, slice(0, D), out_part, 1), (1, slice(0, VEC_COLS), out_part, 2),
                                     (1, slice(VEC_COLS, D), pool_part, 1)):
                sp.wait_ge(part, n)
                sp.dma_start(out_v[t][:, cols], total[:, t, cols]).then_inc(stored, 16)
            sp.wait_ge(stored, 16 * 3)

        @block.gpsimd
        def _(pool):
            nc.gpsimd.memset(ident[:, :], 0.0)
            nc.gpsimd.memset(before[:, :], 1.0).then_inc(zeroed, 1)
            pool.wait_ge(zeroed, 1)
            nc.gpsimd.affine_select(out=ident[:, :], in_=ident[:, :], compare_op=ALU.not_equal, fill=1.0,
                                    base=0, pattern=[[-1, P]], channel_multiplier=1)
            nc.gpsimd.affine_select(out=before[:, :], in_=before[:, :], compare_op=ALU.is_gt, fill=0.0,
                                    base=0, pattern=[[1, P]], channel_multiplier=-1)
            nc.gpsimd.memset(eps[:, :], EPS).then_inc(consts, 1)
            nc.gpsimd.memset(w_a, 0.0)
            nc.gpsimd.memset(w_x, 0.0).then_inc(zeroed, 1)
            pool.dma_start(gain0, io["ln_in_g"].partition_broadcast(P)).then_inc(gain_here[0], 16)
            pool.dma_start(shift0, io["ln_in_b"].partition_broadcast(P)).then_inc(gain_here[0], 16)
            pool.dma_start(router_w[:, :, 0:GROUPS], io["router_group_w"].rearrange("l (k p) g -> (l p) k g", p=P)).then_inc(gates_here, 16)
            pool.dma_start(router_w[:, :, GROUPS:], io["router_expert_w"].rearrange("l (k p) g -> (l p) k g", p=P)).then_inc(gates_here, 16)
            pool.dma_start(router_b[:, 0:GROUPS], io["router_group_b"][0].partition_broadcast(P)).then_inc(gates_here, 16)
            pool.dma_start(router_b[:, GROUPS:], io["router_expert_b"][0].partition_broadcast(P)).then_inc(gates_here, 16)
            pool.wait_ge(zeroed, 2)
            for dst, name in ((w_a, "lru_w_a"), (w_x, "lru_w_x")):
                for b in range(2):
                    src = io[name].rearrange("l (c b) i j -> (l b) i c j", b=2)[b]
                    pool.dma_start(dst[b * HEAD:(b + 1) * HEAD, :, b * HEAD:(b + 1) * HEAD], src).then_inc(gates_here, 16)
            nc.gpsimd.memset(glu[:, :, :, 0:CONF_TAPS - 1], 0.0)
            nc.gpsimd.memset(lru_in[:, :, :, 0:LRU_TAPS - 1], 0.0)
            nc.gpsimd.memset(ones[:, :], 1.0)
            nc.gpsimd.memset(mean_w[:, :], 1.0 / HALF)
            nc.gpsimd.iota(slot_id[:, :, :], pattern=[[1, SEQ]], base=1, channel_multiplier=0,
                           allow_small_or_imprecise_dtypes=True)
            nc.gpsimd.iota(item_no[:, :], pattern=[[1, ITEMS + 1]], base=1, channel_multiplier=0,
                           allow_small_or_imprecise_dtypes=True)
            nc.gpsimd.iota(flag_val[:, 0, :], pattern=[[1, EXPERTS], [0, 3]], base=0, channel_multiplier=0,
                           allow_small_or_imprecise_dtypes=True)
            nc.gpsimd.iota(flag_val[:, 1, :], pattern=[[0, EXPERTS], [1, 3]], base=1, channel_multiplier=0,
                           allow_small_or_imprecise_dtypes=True)
            nc.gpsimd.iota(rt[:, 0:EXPERTS], pattern=[[1, EXPERTS]], base=0, channel_multiplier=0,
                           allow_small_or_imprecise_dtypes=True).then_inc(consts, 1)

            def lower_w(j):
                pool.wait_ge(w_hi_ready, j + 1)
                nc.gpsimd.tensor_tensor(split_part(w_lo, j), raw_part(j), split_part(w_hi, j), ALU.subtract).then_inc(w_lo_ready, 1)

            lower_w(0)
            for f in range(0, 4 * TT, 2):
                pool.wait_ge(hi_act, f // 2 + 1)
                part = bank_part(f)
                ins = nc.gpsimd.tensor_tensor(part_lo[part], h_in_t[part], part_hi[part], ALU.subtract)
            ins.then_inc(h_lo_ready, 1)
            for j in range(1, 2 * (len(IN_ORDER) + OUT_CHUNKS)):
                lower_w(j)
                if j == 2 * len(IN_ORDER) + 3:
                    pool.wait_ge(mix_lo, 2)
                    pool.dma_start(gain1, io["ln1_g"][0].partition_broadcast(P)).then_inc(gain_here[1], 16)
                    pool.dma_start(shift1, io["ln1_b"][0].partition_broadcast(P)).then_inc(gain_here[1], 16)
            pool.wait_ge(gain_here[1], 32)
            for t in range(TT):
                pool.wait_ge(norm_ready, TT + t + 1)
                pool.wait_ge(h2_turned, 4 * (t + 1))
                nc.gpsimd.tensor_tensor(rows[:, t, :], rows[:, t, :], gain1, ALU.mult).then_inc(h2_gained, 1)
            pool.wait_ge(h2_gained, TT)
            nc.gpsimd.tensor_tensor(rows[:, TT - 1, :], rows[:, TT - 1, :], shift1, ALU.add).then_inc(h2_ready, 1)
            for t in range(TT):
                pool.wait_ge(h2_ready, TT)
                ins = nc.gpsimd.tensor_scalar(out=total[:, t, :], in0=rows[:, t, :], scalar1=ALPHA, scalar2=0.0,
                                              op0=ALU.mult, op1=ALU.add)
            ins.then_inc(total_ready, 1)
            rest = total[:, TT - 1, VEC_COLS:]
            pool.wait_ge(gain_here[2], 32)
            pool.wait_ge(last_scaled, 1)
            nc.gpsimd.tensor_tensor(rest, rest, gain2[:, VEC_COLS:], ALU.mult).then_inc(pool_gained, 1)
            pool.wait_ge(pool_gained, 1)
            nc.gpsimd.tensor_tensor(rest, rest, shift2[:, VEC_COLS:], ALU.add).then_inc(pool_part, 1)

        @block.scalar
        def _(act):
            def load_rows(dst, name, r, n, done):
                src = io[name]
                src = src.rearrange("(c q) -> c q", q=P) if len(src.shape) == 1 else (
                    src.rearrange("l (c q) -> (l c) q", q=P) if len(src.shape) == 2 else
                    src.rearrange("l k (c q) -> (l k c) q", q=P))
                act.dma_start(dst[r:r + n, :], src).then_inc(done, 16)

            for name, r in (("ln_in_g", N_G0), ("ln_in_b", N_B0), ("ln1_g", N_G1), ("ln1_b", N_B1)):
                load_rows(raw_n, name, r, KD, norm_here)
            for name, r, n in (("lru_conv_w", R_LCW, LRU_TAPS * CT), ("lru_conv_b", R_LCB, CT), ("lru_b_a", R_BA, CT),
                               ("lru_b_x", R_BX, CT), ("lru_lambda", R_LAM, CT), ("conf_conv_b", R_CCB, CT),
                               ("conf_ln_g", R_CLG, CT), ("conf_ln_b", R_CLB, CT)):
                load_rows(raw_a, name, r, n, params_here)
            taps = io["conf_conv_w"].rearrange("l k (c q) -> (l k c) q", q=P)
            act.dma_start(raw_t[:, 0, :], taps[0:P]).then_inc(params_here, 16)
            act.dma_start(raw_t[0:TAP_ROWS - P, 1, :], taps[P:TAP_ROWS]).then_inc(params_here, 16)

            act.wait_ge(consts, 1)
            for t in range(TT):
                act.wait_ge(var_ready, t + 1)
                nc.scalar.activation(rstd[:, t:t + 1], moments[:, t, 1:2], ACT.Sqrt, bias=eps[:, 0:1]).then_inc(root_ready, 1)

            def upper_w(j):
                if j % 2 == 0:
                    i = j // 2
                    act.wait_ge(chunk_here[i % RAW], 16 * (i // RAW + 1))
                if j >= 2:
                    act.wait_ge(w_used, j - 1)
                nc.scalar.copy(split_part(w_hi, j), raw_part(j)).then_inc(w_hi_ready, 1)

            act.wait_ge(norm_turned, 1)
            nc.scalar.copy(norm_p[:, :], psum[:, 3, 0:ROWS_N]).then_inc(norm_p_ready, 1)
            act.wait_ge(norm_p_ready, 1)

            def even_banks(dst, turned_sem, done, g, b, split=False):
                for f in range(0, 4 * TT, 2):
                    act.wait_ge(turned_sem, f + 1)
                    for k in range(4):
                        kk = 4 * (f % 4) + k
                        ins = nc.scalar.activation(dst[:, kk, (f // 4) * P:(f // 4 + 1) * P], psum[:, 4 + f % 4, k * P:(k + 1) * P],
                                                   ACT.Identity, bias=norm_p[:, b + kk:b + kk + 1],
                                                   scale=norm_p[:, g + kk:g + kk + 1])
                    ins.then_inc(done, 1)
                    if split:
                        act.wait_ge(done, f // 2 + 1)
                        part = bank_part(f)
                        nc.scalar.copy(part_hi[part], dst[part]).then_inc(hi_act, 1)

            upper_w(0)
            even_banks(h_in_t, h_turned, ht_act, N_G0, N_B0, split=True)
            upper_w(1)
            act.wait_ge(params_turned, 1)
            nc.scalar.copy(chan, psum[:, 7, 0:ROWS_A + TAP_ROWS]).then_inc(chan_ready, 1)
            act.wait_ge(chan_ready, 1)
            act.wait_ge(rates_in, 1)
            nc.scalar.activation(decay[:, 1, :], decay[:, 0, :], ACT.Exp).then_inc(rates_exp, 1)

            def conf_gate(i):
                act.wait_ge(w_used, 2 * chunk_no("gate", i) + 2)
                if i >= 2:
                    act.wait_ge(glu_ready, i - 1)
                nc.scalar.activation(conf_sig[:, i % 2], chunk_bank("gate", i), ACT.Sigmoid).then_inc(conf_sig_ready, 1)

            def lru_take(i):
                act.wait_ge(w_used, 2 * chunk_no("x", i) + 2)
                if i >= 2:
                    act.wait_ge(a_in_ready, i - 1)
                nc.scalar.copy(lru_in[:, i % 2, :, LRU_TAPS - 1:], chunk_bank("x", i)).then_inc(lru_in_ready, 1)

            def lru_gelu(i):
                act.wait_ge(w_used, 2 * chunk_no("g", i) + 2)
                if i >= 2:
                    act.wait_ge(lru_done, i - 1)
                nc.scalar.activation(gelu[:, i % 2], chunk_bank("g", i), ACT.Gelu_apprx_tanh).then_inc(gelu_ready, 1)

            def lru_decays(i):
                act.wait_ge(gates_ready, i + 1)
                if i >= 1:
                    act.wait_ge(state_ready, i)
                for c in range(2):
                    cc = 2 * i + c
                    nc.scalar.activation(r_gate[:, c], psum[:, 4, c * SEQ:(c + 1) * SEQ], ACT.Sigmoid,
                                         bias=chan[:, R_BA + cc:R_BA + cc + 1]).then_inc(sca, 1)
                    nc.scalar.activation(i_gate[:, c], psum[:, 5, c * SEQ:(c + 1) * SEQ], ACT.Sigmoid,
                                         bias=chan[:, R_BX + cc:R_BX + cc + 1]).then_inc(sca, 1)
                if i == 0:
                    act.wait_ge(rates_ready, 1)
                act.wait_ge(sca, 6 * i + 4)
                for c in range(2):
                    cc = 2 * i + c
                    nc.scalar.activation(a_dec[:, c], r_gate[:, c], ACT.Exp, scale=decay[:, 7, cc:cc + 1]).then_inc(sca, 1)
                    nc.scalar.activation(a_th[:, c], r_gate[:, c], ACT.Tanh, scale=decay[:, 6, cc:cc + 1])
                act.wait_ge(sca, 6 * i + 6)
                nc.scalar.activation(a_sq, a_dec, ACT.Square).then_inc(decays_ready, 1)

            def lru_root(i):
                act.wait_ge(gap_ready, i + 1)
                nc.scalar.activation(a_th, a_sq, ACT.Sqrt).then_inc(scale_ready, 1)

            def conf_square():
                act.wait_ge(centred, 1)
                nc.scalar.activation(square, conv, ACT.Square).then_inc(square_ready, 1)

            def conf_deviation():
                act.wait_ge(cvar_ready, 1)
                nc.scalar.activation(conf_rstd, psum[:, 7, 0:SEQ], ACT.Sqrt, bias=eps[:, 0:1]).then_inc(conf_root, 1)

            def upper_halves(first, last):
                for j in range(first, last + 1):
                    upper_w(j)

            upper_halves(2, 5)
            conf_gate(0)
            upper_halves(6, 9)
            conf_gate(1)
            upper_halves(10, 11)
            lru_take(0)
            upper_halves(12, 13)
            lru_gelu(0)
            upper_halves(14, 17)
            conf_gate(2)
            upper_w(18)
            lru_decays(0)
            upper_halves(19, 21)
            conf_gate(3)
            upper_halves(22, 23)
            lru_take(1)
            lru_root(0)
            upper_halves(24, 25)
            lru_gelu(1)
            upper_w(26)
            lru_decays(1)
            upper_w(27)
            lru_take(2)
            upper_halves(28, 29)
            lru_take(3)
            lru_root(1)
            lru_decays(2)
            conf_square()
            lru_root(2)
            upper_halves(30, 31)
            lru_gelu(2)
            conf_deviation()
            lru_decays(3)
            first_out = 2 * len(IN_ORDER)
            upper_w(first_out)
            lru_root(3)
            lru_gelu(3)
            act.wait_ge(conf_normed, 1)
            for c in range(CT):
                ins = nc.scalar.activation(mix_t[:, CT + c, :], conv[:, c], ACT.Silu, bias=chan[:, R_CLB + c:R_CLB + c + 1],
                                           scale=chan[:, R_CLG + c:R_CLG + c + 1])
            ins.then_inc(conf_done, 1)
            for j in range(first_out + 1, first_out + 2 * OUT_CHUNKS):
                upper_w(j)

            for t in range(TT):
                act.wait_ge(var_ready, TT + t + 1)
                nc.scalar.activation(rstd[:, t:t + 1], moments[:, t, 1:2], ACT.Sqrt, bias=eps[:, 0:1]).then_inc(root_ready, 1)
            even_banks(h_t, h2_turned, h2t_act, N_G1, N_B1)
            act.wait_ge(logits_t, 1)
            for t in range(TT):
                at = slice(t * SLOTS, t * SLOTS + GROUPS + EXPERTS)
                ins = nc.scalar.copy(router_t[at, :], psum[at, t, 0:P])
            ins.then_inc(logits_copied, 1)
            act.wait_ge(exps_in, 1)
            nc.scalar.activation(rt[:, 480:490], rt[:, 470:480], ACT.Exp).then_inc(exps_ready, 1)

            nc.scalar.activation(sig[:, 0:1], eps[:, :], ACT.Silu)

            def take_quarter(n, q):
                act.wait_ge(xg_gathered, n * QUARTERS + q + 1)
                bank = gather_bank(n, q)
                nc.scalar.copy(xg[:, q * 4:(q + 1) * 4, :], psum[:, bank, :].rearrange(
                    "p (k s) -> p k s", k=4)).then_inc(xg_copied, 1)

            def take_place(n, parity):
                act.wait_ge(place_turned, n + 1)
                nc.scalar.copy(place[:, parity, :], psum[:, 2, 0:SEQ]).then_inc(place_copied, 1)

            def silu(n, e):
                act.wait_ge(gu_used, (n * 2 + e + 1) * GU_PIECES)
                nc.scalar.activation(sig, psum[:, 1, 0:F // 2], ACT.Silu).then_inc(silu_done, 1)

            def take_hid(n, e):
                act.wait_ge(hid_turned, n * 2 + e + 1)
                nc.scalar.copy(hid_t[:, e], psum[:, 2, 0:2 * P].rearrange("p (c s) -> p c s", c=2)).then_inc(hid_copied, 1)

            for q in range(QUARTERS):
                take_quarter(0, q)
            take_place(0, 0)
            with act.Fori(0, LOOPS) as g:
                for u in range(UNROLL):
                    n = g * UNROLL + u
                    silu(n, 0)
                    take_hid(n, 0)
                    silu(n, 1)
                    take_quarter(n + 1, 0)
                    take_hid(n, 1)
                    for q in range(1, QUARTERS):
                        take_quarter(n + 1, q)
                    take_place(n + 1, (u + 1) % 2)
                    for i in range(4):
                        act.wait_ge(y_done, n * 4 + i + 1)
                        nc.scalar.copy(y_sb[:, i], psum[:, 4 + i, :]).then_inc(y_copied, 1)

            act.wait_ge(items_ready, 1)
            n_items = act.value_load(items[0:1, 0, 0:1], min_val=0, max_val=ITEMS)

            def item(i):
                act.wait_ge(i_gu, i + 1)
                nc.scalar.activation(sig, psum[:, 1, 0:F // 2], ACT.Silu).then_inc(i_silu, 1)
                act.wait_ge(i_hid_turned, i + 1)
                nc.scalar.copy(hid_t[:, 0], psum[:, 2, 0:2 * P].rearrange("p (c s) -> p c s", c=2)).then_inc(i_hid_copied, 1)
                with act.If(n_items > i + 1):
                    for q in range(QUARTERS):
                        take_quarter(NPAIRS + 1 + i, q)
                for c in range(4):
                    act.wait_ge(i_down, i * 4 + c + 1)
                    nc.scalar.copy(y_sb[:, c], psum[:, 4 + c, :]).then_inc(i_y, 1)
                with act.If(n_items > i + 1):
                    take_place(NPAIRS + 1 + i, 0)

            with act.If(n_items > 0):
                item(0)
            with act.If(n_items > 1):
                with act.Fori(1, ITEMS) as i:
                    with act.If(n_items > i):
                        item(i)

            for t in range(TT):
                act.wait_ge(var_ready, 2 * TT + t + 1)
                nc.scalar.activation(rstd[:, t:t + 1], moments[:, t, 1:2], ACT.Sqrt, bias=eps[:, 0:1]).then_inc(root_ready, 1)
            act.wait_ge(rstd_ready, 2)
            rest = total[:, TT - 1, VEC_COLS:]
            nc.scalar.activation(rest, rest, ACT.Identity, bias=offset[:, 0:1], scale=rstd[:, TT - 1:TT]).then_inc(last_scaled, 1)

        @block.vector
        def _(dve):
            steps = [0]

            def step(ins):
                steps[0] += 1
                ins.then_inc(vec, 1)
                return steps[0]

            def link(ins):
                dve.wait_ge(vec, step(ins))

            V = nc.vector

            def moments_of(t, src, pieces, width):
                for i in range(pieces):
                    link(V.bn_stats(out=stats[:, t, i, :], in_=src[:, t, i * width:(i + 1) * width]))
                aggregate(t, pieces)

            def aggregate(t, pieces):
                V.bn_aggr(out=moments[:, t, :], in_=stats[:, t, 0:pieces, :].rearrange("p a b -> p (a b)")).then_inc(var_ready, 1)

            def standardise(t, n, src):
                dve.wait_ge(root_ready, n)
                link(V.reciprocal(rstd[:, t:t + 1], rstd[:, t:t + 1]))
                return V.tensor_scalar(out=src[:, t, :], in0=src[:, t, :], scalar1=moments[:, t, 0:1],
                                       scalar2=rstd[:, t:t + 1], op0=ALU.subtract, op1=ALU.mult)

            for t in range(TT):
                dve.wait_ge(x_here[t], 16)
                moments_of(t, rows, 4, 512)
            for t in range(TT):
                standardise(t, t + 1, rows).then_inc(norm_ready, 1)

            def odd_banks(dst, turned_sem, done, g, b, split=False):
                for f in range(1, 4 * TT, 2):
                    dve.wait_ge(turned_sem, f + 1)
                    for k in range(4):
                        kk = 4 * (f % 4) + k
                        ins = V.tensor_scalar(out=dst[:, kk, (f // 4) * P:(f // 4 + 1) * P], in0=psum[:, 4 + f % 4, k * P:(k + 1) * P],
                                              scalar1=norm_p[:, g + kk:g + kk + 1], scalar2=norm_p[:, b + kk:b + kk + 1],
                                              op0=ALU.mult, op1=ALU.add)
                    ins.then_inc(done, 1)
                    if split:
                        dve.wait_ge(done, f // 2 + 1)
                        part = bank_part(f)
                        V.tensor_copy(part_hi[part], dst[part]).then_inc(hi_vec, 1)

            dve.wait_ge(norm_p_ready, 1)
            odd_banks(h_in_t, h_turned, ht_vec, N_G0, N_B0, split=True)
            dve.wait_ge(hi_vec, 4)
            for f in range(1, 4 * TT, 2):
                part = bank_part(f)
                ins = V.tensor_tensor(part_lo[part], h_in_t[part], part_hi[part], ALU.subtract)
            ins.then_inc(h_lo_ready, 1)

            dve.wait_ge(gain_here[0], 32)
            dve.wait_ge(norm_ready, TT)
            for t in range(TT):
                m = step(V.tensor_tensor(rows[:, t, :], rows[:, t, :], gain0, ALU.mult))
            dve.wait_ge(vec, m)
            for t in range(TT):
                m = step(V.tensor_tensor(rows[:, t, :], rows[:, t, :], shift0, ALU.add))
            dve.wait_ge(vec, m)

            lam = chan[:, R_LAM:R_LAM + CT]
            dve.wait_ge(chan_ready, 1)
            V.scalar_tensor_tensor(out=decay[:, 0, :], in0=lam, scalar=-1.0, in1=lam, op0=ALU.mult, op1=ALU.min).then_inc(rates_in, 1)
            dve.wait_ge(rates_exp, 1)
            link(V.tensor_scalar(out=decay[:, 2, :], in0=decay[:, 1, :], scalar1=2.0, scalar2=None, op0=ALU.add))
            link(V.reciprocal(decay[:, 2, :], decay[:, 2, :]))
            link(V.tensor_tensor(decay[:, 2, :], decay[:, 2, :], decay[:, 1, :], ALU.mult))
            link(V.tensor_tensor(decay[:, 3, :], decay[:, 2, :], decay[:, 2, :], ALU.mult))
            link(V.tensor_scalar(out=decay[:, 4, :], in0=decay[:, 3, :], scalar1=1.0 / 17, scalar2=None, op0=ALU.mult))
            for n in range(15, 1, -2):
                link(V.scalar_tensor_tensor(out=decay[:, 4, :], in0=decay[:, 4, :], scalar=1.0 / n, in1=decay[:, 3, :],
                                            op0=ALU.add, op1=ALU.mult))
            link(V.scalar_tensor_tensor(out=decay[:, 4, :], in0=decay[:, 4, :], scalar=1.0, in1=decay[:, 2, :],
                                        op0=ALU.add, op1=ALU.mult))
            link(V.tensor_scalar(out=decay[:, 5, :], in0=lam, scalar1=-1.0, scalar2=0.0, op0=ALU.mult, op1=ALU.max))
            link(V.scalar_tensor_tensor(out=decay[:, 5, :], in0=decay[:, 4, :], scalar=2.0, in1=decay[:, 5, :],
                                        op0=ALU.mult, op1=ALU.add))
            V.tensor_scalar(out=decay[:, 6, :], in0=decay[:, 5, :], scalar1=LRU_C, scalar2=None, op0=ALU.mult)
            V.tensor_scalar(out=decay[:, 7, :], in0=decay[:, 5, :], scalar1=-LRU_C, scalar2=None, op0=ALU.mult).then_inc(rates_ready, 1)

            def taps(dst, src, w_row, b_row, n, i):
                for k in range(n):
                    for c in range(2):
                        cc = 2 * i + c
                        w = chan[:, w_row + k * CT + cc:w_row + k * CT + cc + 1]
                        if k == 0:
                            m = step(V.tensor_scalar(out=dst[c], in0=src[:, c, 0:SEQ], scalar1=w,
                                                     scalar2=chan[:, b_row + cc:b_row + cc + 1], op0=ALU.mult, op1=ALU.add))
                        else:
                            dve.wait_ge(vec, m - 1)
                            m = step(V.scalar_tensor_tensor(out=dst[c], in0=src[:, c, k:k + SEQ], scalar=w, in1=dst[c],
                                                            op0=ALU.mult, op1=ALU.add))
                return m

            dve.wait_ge(consts, 2)

            def conf_conv(i):
                dve.wait_ge(conf_sig_ready, i + 1)
                V.tensor_tensor(glu[:, i % 2, :, CONF_TAPS - 1:], conf_sig[:, i % 2], chunk_bank("value", i), ALU.mult).then_inc(glu_ready, 1)
                dve.wait_ge(glu_ready, i + 1)
                return taps([conv[:, 2 * i + c] for c in range(2)], glu[:, i % 2], R_CCW, R_CCB, CONF_TAPS, i)

            def lru_conv(i):
                dve.wait_ge(lru_in_ready, i + 1)
                b = i % 2
                m = taps([a_in[:, b, c] for c in range(2)], lru_in[:, b], R_LCW, R_LCB, LRU_TAPS - 1, i)
                for c in range(2):
                    cc = 2 * i + c
                    k = LRU_TAPS - 1
                    dve.wait_ge(vec, m - 1 + c)
                    ins = V.scalar_tensor_tensor(out=a_in[:, b, c], in0=lru_in[:, b, c, k:k + SEQ],
                                                 scalar=chan[:, R_LCW + k * CT + cc:R_LCW + k * CT + cc + 1],
                                                 in1=a_in[:, b, c], op0=ALU.mult, op1=ALU.add)
                ins.then_inc(a_in_ready, 1)

            def lru_drive(i):
                b = i % 2
                dve.wait_ge(decays_ready, i + 1)
                dve.wait_ge(a_in_ready, i + 1)
                V.scalar_tensor_tensor(out=a_sq, in0=a_sq, scalar=1.0, in1=a_th, op0=ALU.add, op1=ALU.mult).then_inc(gap_ready, 1)
                link(V.tensor_tensor(drive, i_gate, a_in[:, b], ALU.mult))

            def lru_back(i):
                b = i % 2
                dve.wait_ge(scale_ready, i + 1)
                link(V.tensor_tensor(drive, drive, a_th, ALU.mult))
                for c in range(2):
                    ins = V.tensor_tensor_scan(out=state[:, c], data0=a_dec[:, c], data1=drive[:, c], initial=0.0,
                                               op0=ALU.mult, op1=ALU.add)
                ins.then_inc(state_ready, 1)
                dve.wait_ge(state_ready, i + 1)
                dve.wait_ge(gelu_ready, i + 1)
                V.tensor_tensor(mix_t[:, 2 * i:2 * i + 2, :], state, gelu[:, b], ALU.mult).then_inc(lru_done, 1)

            def split_mix(first, n):
                part = (slice(None), slice(first, first + n))
                V.tensor_copy(part_hi[part], mix_t[part]).then_inc(mix_hi, 1)
                dve.wait_ge(mix_hi, mix_parts[0] + 1)
                mix_parts[0] += 1
                V.tensor_tensor(part_lo[part], mix_t[part], part_hi[part], ALU.subtract).then_inc(mix_lo, 1)

            mix_parts = [0]
            conf_conv(0)
            conf_conv(1)
            lru_conv(0)
            conf_conv(2)
            lru_drive(0)
            lru_conv(1)
            lru_back(0)
            m = conf_conv(3)
            dve.wait_ge(vec, m)
            V.tensor_copy(decay[:, 0, 0:1], conv[:, CT - 1, 0:1]).then_inc(conv_ready, 1)
            lru_conv(2)
            lru_drive(1)
            lru_back(1)
            dve.wait_ge(mean_ready, 1)
            for c in range(CT):
                ins = V.tensor_tensor(conv[:, c], conv[:, c], psum[:, 6, 0:SEQ], ALU.subtract)
            ins.then_inc(centred, 1)
            lru_drive(2)
            lru_conv(3)
            lru_back(2)
            dve.wait_ge(conf_root, 1)
            dve.wait_ge(centred, 1)
            link(V.reciprocal(conf_rstd, conf_rstd))
            for c in range(CT):
                ins = V.tensor_tensor(conv[:, c], conv[:, c], conf_rstd, ALU.mult)
            ins.then_inc(conf_normed, 1)
            lru_drive(3)
            lru_back(3)
            dve.wait_ge(w_used, 2 * len(IN_ORDER))
            dve.wait_ge(lru_done, PAIRS)
            split_mix(0, CT)
            dve.wait_ge(conf_done, 1)
            split_mix(CT, CT)

            for n in range(OUT_CHUNKS - 1):
                cols = slice(n * CHUNK, (n + 1) * CHUNK)
                dve.wait_ge(w_used, 2 * (len(IN_ORDER) + n) + 2)
                V.scalar_tensor_tensor(out=rows[:, :, cols], in0=rows[:, :, cols], scalar=ALPHA,
                                       in1=psum[:, 2 * (n % 4):2 * (n % 4) + 2, 0:CHUNK],
                                       op0=ALU.mult, op1=ALU.add).then_inc(out_taken, 1)
                dve.wait_ge(out_taken, n + 1)
                for t in range(TT):
                    m = step(V.bn_stats(out=stats[:, t, n, :], in_=rows[:, t, cols]))
            n = OUT_CHUNKS - 1
            cols = slice(n * CHUNK, (n + 1) * CHUNK)
            for t in range(TT):
                if t == 0:
                    dve.wait_ge(tile_done, 1)
                else:
                    dve.wait_ge(w_used, 2 * (len(IN_ORDER) + OUT_CHUNKS))
                V.scalar_tensor_tensor(out=rows[:, t, cols], in0=rows[:, t, cols], scalar=ALPHA,
                                       in1=psum[:, 2 * (n % 4) + t, 0:CHUNK], op0=ALU.mult, op1=ALU.add).then_inc(out_taken, 1)
                dve.wait_ge(out_taken, n + t + 1)
                link(V.bn_stats(out=stats[:, t, n, :], in_=rows[:, t, cols]))
                aggregate(t, 8)
                standardise(t, TT + t + 1, rows).then_inc(norm_ready, 1)
            odd_banks(h_t, h2_turned, h2t_vec, N_G1, N_B1)

            big = 1e30
            at = [EXPERTS]

            def small(*shape):
                n = 1
                for s in shape:
                    n *= s
                a = at[0]
                at[0] = a + n
                assert at[0] <= 470
                v = rt[:, a:a + n]
                if len(shape) == 2:
                    return v.rearrange("p (a b) -> p a b", a=shape[0])
                return v

            number = rt[:, 0:EXPERTS]
            logits = small(TT, GROUPS + EXPERTS)
            top_g = small(TT, 1)
            cand = small(TT, EXPERTS)
            first = small(TT, 1)
            group = small(TT, GROUPS)
            top1 = small(TT, 1)
            top2 = small(TT, 1)
            hot1 = small(TT, EXPERTS)
            hot2 = small(TT, EXPERTS)
            count = small(EXPERTS)[0:1]
            exp_in = rt[:, 470:480].rearrange("p (a b) -> p a b", a=TT)
            exp_out = rt[:, 480:490].rearrange("p (a b) -> p a b", a=TT)
            prob = rt[:, 490:492].rearrange("p (a b) -> p a b", a=TT)
            q1 = rt[:, 492:494].rearrange("p (a b) -> p a b", a=TT)
            q2 = rt[:, 494:496].rearrange("p (a b) -> p a b", a=TT)
            le = logits[:, :, GROUPS:]

            def wide(v, n):
                return v.to_broadcast([P, TT, n])

            def pick_first(dst, src, top, n):
                link(V.tensor_tensor(dst, src, wide(top, n), ALU.is_equal))
                for t in range(TT):
                    m = step(V.scalar_tensor_tensor(out=cand[:, t, 0:n], in0=number[:, 0:n], scalar=-64.0, in1=dst[:, t],
                                                    op0=ALU.add, op1=ALU.mult))
                dve.wait_ge(vec, m)
                link(V.tensor_reduce(out=first, in_=cand[:, :, 0:n], axis=AX.X, op=ALU.min))
                link(V.tensor_tensor(dst, cand[:, :, 0:n], wide(first, n), ALU.is_equal))

            dve.wait_ge(gain_here[1], 32)
            dve.wait_ge(h2_gained, 1)
            V.tensor_tensor(rows[:, 0, :], rows[:, 0, :], shift1, ALU.add).then_inc(h2_ready, 1)
            dve.wait_ge(gates_here, 16 * 8)
            dve.wait_ge(logits_ready, 1)
            link(V.tensor_tensor(logits, psum[:, 2:2 + TT, 0:GROUPS + EXPERTS],
                                 router_b[:, :].unsqueeze(1).to_broadcast([P, TT, GROUPS + EXPERTS]), ALU.add))
            link(V.tensor_reduce(out=top_g, in_=logits[:, :, 0:GROUPS], axis=AX.X, op=ALU.max))
            link(V.tensor_tensor(exp_in[:, :, 0:GROUPS], logits[:, :, 0:GROUPS], wide(top_g, GROUPS), ALU.subtract))
            pick_first(group, logits[:, :, 0:GROUPS], top_g, GROUPS)
            link(V.tensor_scalar(out=group, in0=group, scalar1=-1.0, scalar2=big, op0=ALU.add, op1=ALU.mult))
            for t in range(TT):
                m = step(V.tensor_tensor(le[:, t].rearrange("p (g e) -> p g e", g=GROUPS),
                                         le[:, t].rearrange("p (g e) -> p g e", g=GROUPS),
                                         group[:, t].unsqueeze(2).to_broadcast([P, GROUPS, PER_GROUP]), ALU.add))
            dve.wait_ge(vec, m)
            link(V.tensor_reduce(out=top1, in_=le, axis=AX.X, op=ALU.max))
            pick_first(hot1, le, top1, EXPERTS)
            link(V.scalar_tensor_tensor(out=le, in0=hot1, scalar=-2 * big, in1=le, op0=ALU.mult, op1=ALU.add))
            link(V.tensor_reduce(out=top2, in_=le, axis=AX.X, op=ALU.max))
            V.tensor_tensor(exp_in[:, :, GROUPS:], top2, top1, ALU.subtract).then_inc(exps_in, 1)
            pick_first(hot2, le, top2, EXPERTS)
            V.tensor_tensor(mask, hot2, hot1, ALU.add).then_inc(masks_ready, 1)
            dve.wait_ge(exps_ready, 1)
            link(V.tensor_reduce(out=prob, in_=exp_out[:, :, 0:GROUPS], axis=AX.X, op=ALU.add))
            link(V.reciprocal(prob, prob))
            link(V.tensor_scalar(out=q1, in0=exp_out[:, :, GROUPS:], scalar1=1.0, scalar2=None, op0=ALU.add))
            link(V.reciprocal(q1, q1))
            link(V.tensor_tensor(q2, q1, exp_out[:, :, GROUPS:], ALU.mult))
            link(V.tensor_tensor(q1, q1, prob, ALU.mult))
            link(V.tensor_tensor(q2, q2, prob, ALU.mult))
            link(V.tensor_tensor(weight[:, :, 0:EXPERTS], hot1, wide(q1, EXPERTS), ALU.mult))
            link(V.tensor_tensor(cand, hot2, wide(q2, EXPERTS), ALU.mult))
            link(V.tensor_tensor(weight[:, :, 0:EXPERTS], weight[:, :, 0:EXPERTS], cand, ALU.add))
            dve.wait_ge(masks_ready, 1)
            dve.wait_ge(ranks_ready, 1)
            link(V.scalar_tensor_tensor(out=rank[:, :, 0:EXPERTS], in0=psum[:, 0, 0:TT * EXPERTS].rearrange("p (a b) -> p a b", a=TT),
                                        scalar=1.0, in1=mask, op0=ALU.add, op1=ALU.mult))

            def one_hots(e_cols, w_cols, ids):
                for out_, cols in ((pick, e_cols), (pick_w, w_cols)):
                    for t in range(TT):
                        for e, column in enumerate(cols):
                            kw = dict(scalar2=None) if out_ is pick else dict(scalar2=weight[:, t, column], op1=ALU.mult)
                            ins = V.tensor_scalar(out=out_[:, t, e * SLOTS:(e + 1) * SLOTS], in0=ids, scalar1=rank[:, t, column],
                                                  op0=ALU.is_equal, **kw)
                    ins.then_inc(onehot_ready, 1)

            def pair_hots(n):
                cols = [slice(e, e + 1) if isinstance(n, int) and n == 0 else bass.ds(2 * n + e, 1) for e in range(2)]
                one_hots(cols, cols, slot_id[:, 0, :])

            def item_hots(i):
                expert = dve.value_load(items[0:1, 1, bass.ds(i, 1)], min_val=0, max_val=EXPERTS - 1)
                block_no = dve.value_load(items[0:1, 2, bass.ds(i, 1)], min_val=0, max_val=BLOCKS - 1)
                column = bass.ds(expert, 1)
                one_hots([column], [column, column], slot_id[:, bass.ds(block_no, 1), :].rearrange("p o s -> p (o s)"))

            def add_round(n, r, bank=3, stat=False):
                t, q = r // 4, r % 4
                dve.wait_ge(scattered, n * ROUNDS + r + 1)
                dst = total[:, t, q * 512:(q + 1) * 512]
                V.tensor_tensor(dst, dst, psum[:, bank, :], ALU.add).then_inc(added, 1)
                if stat:
                    dve.wait_ge(added, n * ROUNDS + r + 1)
                    V.bn_stats(out=stats[:, t, q, :], in_=dst).then_inc(stat_done, 1)

            def hidden(n, e):
                dve.wait_ge(silu_done, n * 2 + e + 1)
                V.tensor_tensor(hid[:, e], sig, psum[:, 1, F // 2:F], ALU.mult).then_inc(hid_ready, 1)

            def body(g, first=False, last=False):
                for u in range(UNROLL):
                    n = g * UNROLL + u
                    adds = not (first and u == 0)
                    dve.wait_ge(place_turned, n + 1)
                    if last and u == UNROLL - 1:
                        item_hots(0)
                    else:
                        pair_hots(n + 1)
                    for e in range(2):
                        for r in range(4):
                            if r == 3:
                                hidden(n, e)
                            if adds:
                                add_round(n - 1, 4 * e + r)

            dve.wait_ge(vec, steps[0])
            pair_hots(0)
            link(V.tensor_copy(count, psum[0:1, 3, 0:EXPERTS]))

            for b in range(1, BLOCKS):
                m = step(V.tensor_scalar(out=flags[:, 0, :].rearrange("p (e b) -> p e b", b=3)[:, :, b - 1:b],
                                         in0=count.unsqueeze(2), scalar1=SLOTS * b + 0.5, scalar2=None,
                                         op0=ALU.is_gt))
            dve.wait_ge(vec, m)
            link(V.tensor_tensor_scan(out=flags[:, 1, :], data0=ones[0:1, 0:3 * EXPERTS], data1=flags[:, 0, :], initial=0.0,
                                      op0=ALU.mult, op1=ALU.add))
            link(V.tensor_tensor(flags[:, 1, :], flags[:, 1, :], flags[:, 0, :], ALU.mult))
            for i in range(ITEMS + 1):
                link(V.tensor_scalar(out=flags[:, 2, :], in0=flags[:, 1, :], scalar1=item_no[:, i:i + 1], scalar2=None,
                                     op0=ALU.is_equal))
                for v in range(2):
                    link(V.tensor_tensor(flags[:, 3, :], flags[:, 2, :], flag_val[:, v, :], ALU.mult))
                    link(V.tensor_reduce(out=items[:, 1 + v, i:i + 1], in_=flags[:, 3, :], axis=AX.X, op=ALU.max))
            V.tensor_reduce(out=items[:, 0, 0:1], in_=flags[:, 1, :], axis=AX.X, op=ALU.max).then_inc(items_ready, 1)

            dve.wait_ge(total_ready, 1)
            body(0, first=True)
            with dve.Fori(1, LOOPS - 1) as g:
                body(g)
            body(LOOPS - 1, last=True)
            for r in range(ROUNDS):
                add_round(NPAIRS - 1, r, bank=END_BANKS[r % 3], stat=True)

            dve.wait_ge(items_ready, 1)
            n_items = dve.value_load(items[0:1, 0, 0:1], min_val=0, max_val=ITEMS)

            def item(i):
                with dve.If(n_items > i + 1):
                    dve.wait_ge(place_turned, NPAIRS + 1 + i)
                    item_hots(i + 1)
                dve.wait_ge(i_silu, i + 1)
                V.tensor_tensor(hid[:, 0], sig, psum[:, 1, F // 2:F], ALU.mult).then_inc(i_hid, 1)
                for r in range(ROUNDS + 1):
                    if r < ROUNDS:
                        dve.wait_ge(i_scattered, i * ROUNDS + r + 1)
                        dst = total[:, r // 4, r % 4 * 512:(r % 4 + 1) * 512]
                        V.tensor_tensor(dst, dst, psum[:, ITEM_BANKS[r % 3], :], ALU.add).then_inc(i_added, 1)
                    if r >= 1:
                        dve.wait_ge(i_added, i * ROUNDS + r)
                        t, c = (r - 1) // 4, (r - 1) % 4
                        V.bn_stats(out=stats[:, t, c, :], in_=total[:, t, c * 512:(c + 1) * 512]).then_inc(stat_done, 1)

            with dve.If(n_items > 0):
                item(0)
            with dve.If(n_items > 1):
                with dve.Fori(1, ITEMS) as i:
                    with dve.If(n_items > i):
                        item(i)

            V.tensor_copy(count[:, 0:1], count[:, 0:1]).then_inc(stats_seen, 1)
            dve.wait_ge(stats_seen, 1)
            for t in range(TT):
                aggregate(t, 4)
            dve.wait_ge(gain_here[2], 32)
            dve.wait_ge(root_ready, 3 * TT)
            V.reciprocal(rstd[:, :], rstd[:, :]).then_inc(rstd_ready, 1)
            dve.wait_ge(rstd_ready, 1)
            V.scalar_tensor_tensor(out=offset[:, :], in0=moments[:, TT - 1, 0:1], scalar=-1.0, in1=rstd[:, TT - 1:TT],
                                   op0=ALU.mult, op1=ALU.mult).then_inc(rstd_ready, 1)
            for t, cols in ((0, slice(0, D)), (1, slice(0, VEC_COLS))):
                V.scalar_tensor_tensor(out=total[:, t, cols], in0=total[:, t, cols], scalar=moments[:, t, 0:1],
                                       in1=gain2[:, cols], op0=ALU.subtract, op1=ALU.mult).then_inc(gained, 1)
                dve.wait_ge(gained, t + 1)
                V.scalar_tensor_tensor(out=total[:, t, cols], in0=total[:, t, cols], scalar=rstd[:, t:t + 1],
                                       in1=shift2[:, cols], op0=ALU.mult, op1=ALU.add).then_inc(out_part, 1)

        @block.tensor
        def _(pe):
            def mm(dst, lhs, rhs, first, last):
                return nc.tensor.matmul(dst, lhs, rhs, start=first, stop=last)

            pe.wait_ge(consts, 1)
            pe.wait_ge(norm_here, 16 * 4)
            nc.tensor.transpose(psum[:, 3, 0:ROWS_N], raw_n[:, :], ident[0:ROWS_N, 0:ROWS_N]).then_inc(norm_turned, 1)

            def turn_rows(ready, base, done):
                for f in range(8):
                    if f % 4 == 0:
                        pe.wait_ge(ready, base + f // 4 + 1)
                    if f == 3 and done is h2_turned:
                        pe.wait_ge(out_taken, OUT_CHUNKS + 1)
                    if f >= 4:
                        if f % 2 == 0:
                            pe.wait_ge(ht_act if done is h_turned else h2t_act, (f - 4) // 2 + 1)
                        else:
                            pe.wait_ge(ht_vec if done is h_turned else h2t_vec, (f - 4) // 2 + 1)
                    for k in range(4):
                        kk = 4 * (f % 4) + k
                        ins = nc.tensor.transpose(psum[:, 4 + f % 4, k * P:(k + 1) * P],
                                                  rows[:, f // 4, kk * P:(kk + 1) * P], ident[:, :])
                    ins.then_inc(done, 1)

            turn_rows(norm_ready, 0, h_turned)
            pe.wait_ge(params_here, 16 * 10)
            pe.wait_ge(ht_vec, 4)
            nc.tensor.transpose(psum[:, 7, 0:ROWS_A], raw_a[0:ROWS_A, :], ident[0:ROWS_A, 0:ROWS_A])
            nc.tensor.transpose(psum[:, 7, ROWS_A:ROWS_A + P], raw_t[:, 0, :], ident[:, :])
            n = TAP_ROWS - P
            nc.tensor.transpose(psum[:, 7, ROWS_A + P:ROWS_A + TAP_ROWS], raw_t[0:n, 1, :], ident[0:n, 0:n]).then_inc(params_turned, 1)
            pe.wait_ge(hi_act, 4)
            pe.wait_ge(hi_vec, 4)

            def project(i):
                if i >= 4:
                    q, j = IN_ORDER[i - 4]
                    pe.wait_ge({"value": glu_ready, "gate": conf_sig_ready, "x": lru_in_ready, "g": gelu_ready}[q], j + 1)
                for c in range(2):
                    j = 2 * i + c
                    pe.wait_ge(w_hi_ready, j + 1)
                    for n, (w, part) in enumerate(((w_hi, part_hi), (w_hi, part_lo), (w_lo, part_hi))):
                        if n == 1 and j == 0:
                            pe.wait_ge(h_lo_ready, 2)
                        if n == 2:
                            pe.wait_ge(w_lo_ready, j + 1)
                        for k in range(KD):
                            ins = mm(psum[:, i % 4, c * SEQ:(c + 1) * SEQ], split_part(w, j)[:, k, :], part[:, k, :],
                                     n == 0 and k == 0, n == 2 and k == KD - 1)
                    ins.then_inc(w_used, 1)

            def lru_gates(i):
                pe.wait_ge(a_in_ready, i + 1)
                if i >= 1:
                    pe.wait_ge(decays_ready, i)
                for bank, w in ((4, w_a), (5, w_x)):
                    for c in range(2):
                        ins = mm(psum[:, bank, c * SEQ:(c + 1) * SEQ], w[:, 2 * i + c, :], a_in[:, i % 2, c], True, True)
                ins.then_inc(gates_ready, 1)

            def channel_mean(bank, src):
                for c in range(CT):
                    ins = mm(psum[:, bank, 0:SEQ], mean_w[:, :], src[:, c], c == 0, c == CT - 1)
                return ins

            for i, (q, j) in enumerate(IN_ORDER):
                project(i)
                if (q, j) == ("gate", 2):
                    pe.wait_ge(gates_here, 16 * 8)
                    lru_gates(0)
                elif (q, j) == ("g", 1):
                    lru_gates(1)
                elif (q, j) == ("x", 3):
                    lru_gates(2)
                    pe.wait_ge(conv_ready, 1)
                    channel_mean(6, conv).then_inc(mean_ready, 1)
                elif (q, j) == ("g", 2):
                    pe.wait_ge(square_ready, 1)
                    channel_mean(7, square).then_inc(cvar_ready, 1)
                    lru_gates(3)

            for n in range(OUT_CHUNKS):
                i = len(in_cols) + n
                if n >= 4:
                    pe.wait_ge(out_taken, n - 3)
                elif n == 0:
                    pe.wait_ge(lru_in_ready, PAIRS)
                elif n == 1:
                    pe.wait_ge(gelu_ready, PAIRS)
                elif n == 2:
                    pe.wait_ge(decays_ready, PAIRS)
                else:
                    pe.wait_ge(conf_root, 1)
                for b in range(2):
                    j = 2 * i + b
                    pe.wait_ge(w_hi_ready, j + 1)
                    pe.wait_ge(mix_hi, b + 1)
                    products = ((part_hi, w_hi), (part_lo, w_hi), (part_hi, w_lo))
                    by_tile = n == OUT_CHUNKS - 1 and b == 1
                    for m, t in ([(m, t) for t in range(TT) for m in range(3)] if by_tile else
                                 [(m, t) for m in range(3) for t in range(TT)]):
                        part, w = products[m]
                        if m == 1:
                            pe.wait_ge(mix_lo, b + 1)
                        if m == 2:
                            pe.wait_ge(w_lo_ready, j + 1)
                        for k in range(CT):
                            ins = mm(psum[:, 2 * (n % 4) + t, 0:CHUNK], part[:, b * CT + k, t * P:(t + 1) * P],
                                     split_part(w, j)[:, k, :], b == 0 and m == 0 and k == 0,
                                     b == 1 and m == 2 and k == CT - 1)
                        if by_tile and m == 2 and t == 0:
                            ins.then_inc(tile_done, 1)
                    ins.then_inc(w_used, 1)

            n = GROUPS + EXPERTS
            turn_rows(norm_ready, TT, h2_turned)
            for k in range(KD):
                if k % 4 == 0:
                    pe.wait_ge(h2t_vec if k // 4 % 2 else h2t_act, k // 8 + 3)
                for t in range(TT):
                    ins = mm(psum[t * SLOTS:t * SLOTS + n, t, 0:P], router_w[:, k, :], h_t[:, k, t * P:(t + 1) * P], k == 0, k == KD - 1)
            ins.then_inc(logits_t, 1)
            pe.wait_ge(logits_copied, 1)
            for t in range(TT):
                at = slice(t * SLOTS, t * SLOTS + n)
                ins = nc.tensor.transpose(psum[:, 2 + t, 0:n], router_t[at, :], ident[at, at])
            ins.then_inc(logits_ready, 1)
            pe.wait_ge(masks_ready, 1)
            mm(psum[:, 0, 0:EXPERTS], before[:, :], mask[:, 0], True, True)
            mm(psum[:, 0, EXPERTS:2 * EXPERTS], before[:, :], mask[:, 1], True, False)
            mm(psum[:, 0, EXPERTS:2 * EXPERTS], ones[:, :], mask[:, 0], False, True)
            mm(psum[:, 3, 0:EXPERTS], ones[:, :], mask[:, 0], True, False)
            mm(psum[:, 3, 0:EXPERTS], ones[:, :], mask[:, 1], False, True).then_inc(ranks_ready, 1)

            def gather(n, q):
                if q == 0:
                    pe.wait_ge(onehot_ready, 2 * n + 1)
                bank = gather_bank(n, q)
                if isinstance(n, int) and n == 0:
                    pe.wait_ge(h2_ready, TT)
                else:
                    pe.wait_ge(xg_copied, n * QUARTERS + q)
                for k in range(4):
                    kk = 4 * q + k
                    for t in range(TT):
                        ins = mm(psum[:, bank, k * P:(k + 1) * P], rows[:, t, kk * P:(kk + 1) * P], pick[:, t, :], t == 0, t == TT - 1)
                ins.then_inc(xg_gathered, 1)

            def turn_place(n):
                pe.wait_ge(onehot_ready, 2 * n + 2)
                for t in range(TT):
                    ins = nc.tensor.transpose(psum[:, 2, t * P:(t + 1) * P], pick_w[:, t, :], ident[:, :])
                ins.then_inc(place_turned, 1)

            def scatter_round(n, r, parity, bank=3):
                if r < 4:
                    pe.wait_ge(y_copied, n * 4 + r + 1)
                t, q = r // 4, r % 4
                mm(psum[:, bank, :], place[:, parity, t * P:(t + 1) * P], y_sb[:, q, :], True, True).then_inc(scattered, 1)

            def turn_hid(n, e):
                pe.wait_ge(hid_ready, n * 2 + e + 1)
                for c in range(2):
                    ins = nc.tensor.transpose(psum[:, 2, c * P:(c + 1) * P], hid[:, e, c * P:(c + 1) * P], ident[:, :])
                ins.then_inc(hid_turned, 1)

            def gate_up(slot, k, kk, bank, cols):
                for b in range(2):
                    ins = mm(psum[b * SLOTS:(b + 1) * SLOTS, bank, :], xg[:, kk, cols],
                             gu_slot[slot][:, :, k, b * F // 2:(b + 1) * F // 2], kk == 0, kk == KD - 1)
                return ins

            def body(g, first=False):
                for u in range(UNROLL):
                    n = g * UNROLL + u
                    scatters = not (first and u == 0)

                    def here(q):
                        j = u * PAIR + q
                        s = j % RING
                        pe.wait_ge(arrived[s], g * TURNS * 32 + 32 * (j // RING + 1))
                        return s

                    starts = first and u == 0
                    if starts:
                        gather(0, 0)
                    else:
                        pe.wait_ge(xg_copied, (n + 1) * QUARTERS)
                    for e in range(2):
                        if e == 1:
                            pe.wait_ge(hid_ready, n * 2 + 1)
                        for q in range(GU_PIECES):
                            s = here(e * GU_PIECES + q)
                            if starts and e == 0:
                                pe.wait_ge(xg_copied, q + 1)
                            for k in range(KP):
                                ins = gate_up(s, k, q * KP + k, 1, slice(e * SLOTS, (e + 1) * SLOTS))
                            ins.then_inc(gu_used, 1)
                            if starts and e == 0:
                                for later in {0: (1, 2), 1: (3,)}.get(q, ()):
                                    gather(0, later)
                                if q == 2:
                                    turn_place(0)
                            if scatters:
                                r = e * 4 + q
                                if not (isinstance(g, int) and n == 1 and r == 0):
                                    pe.wait_ge(added, (n - 1) * ROUNDS + r)
                                scatter_round(n - 1, r, (u + 1) % 2)
                            if e == 1 and q == 1:
                                pe.wait_ge(place_copied, n + 1)
                                turn_hid(n, 0)
                    gather(n + 1, 0)
                    pe.wait_ge(hid_copied, n * 2 + 1)
                    turn_hid(n, 1)
                    gather(n + 1, 1)
                    pe.wait_ge(hid_copied, n * 2 + 2)
                    for q in range(DOWN_PIECES):
                        s = [here(2 * GU_PIECES + 2 * q + e) for e in range(2)]

                        def down(c, i):
                            for e in range(2):
                                ins = mm(psum[e * SLOTS:(e + 1) * SLOTS, 4 + i, :], hid_t[:, e, c, q * SLOTS:(q + 1) * SLOTS],
                                         down_slot[s[e]][:, c, i * 512:(i + 1) * 512], q == 0 and c == 0, q == 1 and c == 1)
                            return ins

                        if q == 0:
                            for c in range(2):
                                for i in range(4):
                                    ins = down(c, i)
                                if c == 0:
                                    gather(n + 1, 2)
                            ins.then_inc(down_used, 1)
                            gather(n + 1, 3)
                            turn_place(n + 1)
                        else:
                            for i in range(4):
                                down(0, i)
                                down(1, i).then_inc(y_done, 1)

            body(0, first=True)
            with pe.Fori(1, LOOPS) as g:
                body(g)
            pe.wait_ge(xg_copied, (NPAIRS + 1) * QUARTERS)
            pe.wait_ge(place_copied, NPAIRS + 1)
            pe.wait_ge(items_ready, 1)
            n_items = pe.value_load(items[0:1, 0, 0:1], min_val=0, max_val=ITEMS)

            def item_gate_up(i, q):
                pe.wait_ge(arrived[q], i * 32 + 32 * LOOPS * TURNS + 32)
                for k in range(KP):
                    ins = gate_up(q, k, q * KP + k, 1, slice(0, SLOTS))
                if q == GU_PIECES - 1:
                    ins.then_inc(i_gu, 1)

            def item_rest(i):
                pe.wait_ge(i_hid, i + 1)
                for c in range(2):
                    ins = nc.tensor.transpose(psum[:, 2, c * P:(c + 1) * P], hid[:, 0, c * P:(c + 1) * P], ident[:, :])
                ins.then_inc(i_hid_turned, 1)
                with pe.If(n_items > i + 1):
                    for q in range(QUARTERS):
                        gather(NPAIRS + 1 + i, q)
                pe.wait_ge(i_hid_copied, i + 1)
                for q in range(DOWN_PIECES):
                    s = GU_PIECES + q
                    pe.wait_ge(arrived[s], i * 32 + 32 * LOOPS * TURNS + 32)
                    for c in range(4):
                        for b in range(2):
                            ins = mm(psum[b * SLOTS:(b + 1) * SLOTS, 4 + c, :], hid_t[:, 0, b, q * SLOTS:(q + 1) * SLOTS],
                                     down_slot[s][:, b, c * 512:(c + 1) * 512], q == 0, q == 1)
                        if q == 1:
                            ins.then_inc(i_down, 1)
                for r in range(ROUNDS):
                    t, c = r // 4, r % 4
                    if r < 4:
                        pe.wait_ge(i_y, i * 4 + c + 1)
                    if r >= 3:
                        pe.wait_ge(i_added, i * ROUNDS + r - 2)
                    mm(psum[:, ITEM_BANKS[r % 3], :], place[:, 0, t * P:(t + 1) * P], y_sb[:, c, :], True, True).then_inc(i_scattered, 1)
                with pe.If(n_items > i + 1):
                    turn_place(NPAIRS + 1 + i)
                    pe.wait_ge(xg_copied, (NPAIRS + 2) * QUARTERS + i * QUARTERS)
                    pe.wait_ge(i_added, i * ROUNDS + ROUNDS)

            for q in range(GU_PIECES):
                for r in (2 * q, 2 * q + 1):
                    pe.wait_ge(added, (NPAIRS - 1) * ROUNDS + max(r - 2, 0))
                    scatter_round(NPAIRS - 1, r, (UNROLL - 1) % 2, bank=END_BANKS[r % 3])
                with pe.If(n_items > 0):
                    item_gate_up(0, q)
            with pe.If(n_items > 0):
                pe.wait_ge(added, NPAIRS * ROUNDS)
                item_rest(0)
            with pe.If(n_items > 1):
                with pe.Fori(1, ITEMS) as i:
                    with pe.If(n_items > i):
                        for q in range(GU_PIECES):
                            item_gate_up(i, q)
                        item_rest(i)


INPUTS = ["x", "ln_in_g", "ln_in_b", "w_in", "lru_conv_w", "lru_conv_b", "lru_w_a", "lru_b_a", "lru_w_x", "lru_b_x",
          "lru_lambda", "conf_conv_w", "conf_conv_b", "conf_ln_g", "conf_ln_b", "w_out", "ln1_g", "ln1_b",
          "router_group_w", "router_group_b", "router_expert_w", "router_expert_b", "exp_w_gate", "exp_w_up",
          "exp_w_down", "ln2_g", "ln2_b"]


def kernel(**inputs):
    import numpy as np
    import concourse.bacc as bacc
    from concourse.bass_utils import run_bass_kernel_spmd

    nc = bacc.Bacc("TRN2", target_bir_lowering=False, num_devices=1)
    arrays, io = {}, {}
    for name in INPUTS:
        a = np.ascontiguousarray(inputs[name])
        arrays[f"in_{name}"] = a
        io[name] = nc.dram_tensor(f"in_{name}", a.shape, mybir.dt.from_np(a.dtype), kind="ExternalInput").ap()
    out = nc.dram_tensor("out_0", (1, SEQ, D), mybir.dt.float32, kind="ExternalOutput").ap()
    build(nc, io, out)
    r = run_bass_kernel_spmd(nc, [arrays], core_ids=[0])
    return r.results[0]["out_0"]
```
